# Optimizing a Trainium2 kernel written in Bass

```python
import math
import jax, jax.numpy as jnp
from jax import lax
import numpy as np

D_MODEL = 1024
BATCH = 1
SEQ = 512
DEPTH = 4
DEC_BATCH = 8
DEC_SEQ = 8
PAST_LEN = 1024
PAGE_SIZE = 128

N_MIXERS = 3
N_GMLP_LAYERS = (DEPTH + 2) // 3
N_CONV_LAYERS = (DEPTH + 1) // 3
N_MLA_LAYERS = DEPTH // 3

ALPHA = (2.0 * DEPTH) ** 0.25
BETA = (8.0 * DEPTH) ** -0.25
LN_EPS = 1e-5
RMS_EPS = 1e-6

GMLP_DIM = 2 * D_MODEL
GMLP_GROUPS = 8
GMLP_CHUNK = 128

CONV_WIDTH = 31

MLA_HEADS = 8
MLA_Q_RANK = 384
MLA_KV_RANK = 256
MLA_NOPE = 128
MLA_ROPE = 64
MLA_V = 128
ROPE_THETA = 10000.0
Q_BLOCK = 128
MLA_SCALE = (MLA_NOPE + MLA_ROPE) ** -0.5

FFN_DIM = ((8 * D_MODEL + 3 * 256 - 1) // (3 * 256)) * 256

kernel_name = 'hybrid_gmlp_conformer_mla_adaln_deepnorm_step'

def layer_norm(x, g, b):
    xf = x.astype(jnp.float32)
    mu = jnp.mean(xf, -1, keepdims=True)
    var = jnp.mean(jnp.square(xf - mu), -1, keepdims=True)
    return ((xf - mu) * lax.rsqrt(var + LN_EPS)).astype(x.dtype) * g + b

def rms_norm(x, g):
    xf = x.astype(jnp.float32)
    return (xf * lax.rsqrt(jnp.mean(jnp.square(xf), -1, keepdims=True) + RMS_EPS)).astype(x.dtype) * g

def rope(x, pos):
    half = x.shape[-1] // 2
    inv = ROPE_THETA ** (-jnp.arange(half, dtype=jnp.float32) / half)
    ang = pos.astype(jnp.float32)[:, None] * inv[None, :]
    cos = jnp.cos(ang)[None, :, None, :].astype(x.dtype)
    sin = jnp.sin(ang)[None, :, None, :].astype(x.dtype)
    x1, x2 = x[..., :half], x[..., half:]
    return jnp.concatenate([x1 * cos - x2 * sin, x2 * cos + x1 * sin], -1)

def adaln(c, w, b):
    m = (jax.nn.silu(c) @ w + b).reshape(c.shape[0], 6, 1, D_MODEL)
    return m[:, 0], m[:, 1], m[:, 2], m[:, 3], m[:, 4], m[:, 5]

def swiglu_ffn(h, wg, wu, wd):
    return (jax.nn.silu(h @ wg) * (h @ wu)) @ wd

def gmlp_mixer(h, w_in, ln_g, ln_b, w_s, b_s, w_out):
    bsz, t, _ = h.shape
    z = jax.nn.gelu(h @ w_in, approximate=False)
    u, v = z[..., :GMLP_DIM], z[..., GMLP_DIM:]
    v = layer_norm(v, ln_g, ln_b)
    l = min(t, GMLP_CHUNK)
    n = t // l
    cg = GMLP_DIM // GMLP_GROUPS
    causal = jnp.tril(jnp.ones((l, l), dtype=bool))
    w = jnp.where(causal[None], w_s[:, :l, :l], 0)
    vc = v.reshape(bsz, n, l, GMLP_GROUPS, cg)
    mixed = jnp.einsum('gts,bnsgc->bntgc', w, vc) + b_s[:, :l].T[None, None, :, :, None]
    y = (u * mixed.reshape(bsz, t, GMLP_DIM)) @ w_out
    return y, v

def conv_module(h, ctx, w_pw1, b_pw1, w_dw, b_dw, ln_g, ln_b, w_pw2, b_pw2):
    a = h @ w_pw1 + b_pw1
    a = a[..., :D_MODEL] * jax.nn.sigmoid(a[..., D_MODEL:])
    full = jnp.concatenate([ctx, a], 1)
    y = lax.conv_general_dilated(full, w_dw[:, None, :], window_strides=(1,), padding='VALID',
                                 dimension_numbers=('NWC', 'WIO', 'NWC'),
                                 feature_group_count=D_MODEL) + b_dw
    y = jax.nn.silu(layer_norm(y, ln_g, ln_b))
    return y @ w_pw2 + b_pw2, full[:, -(CONV_WIDTH - 1):]

def mla_project(h, pos, w_down, g_q, g_kv, w_uq, w_uk):
    bsz, t, _ = h.shape
    d = h @ w_down
    q_lat = rms_norm(d[..., :MLA_Q_RANK], g_q)
    ckv = rms_norm(d[..., MLA_Q_RANK:MLA_Q_RANK + MLA_KV_RANK], g_kv)
    kr = rope(d[..., MLA_Q_RANK + MLA_KV_RANK:][:, :, None, :], pos)[:, :, 0]
    q = (q_lat @ w_uq).reshape(bsz, t, MLA_HEADS, MLA_NOPE + MLA_ROPE)
    q_abs = jnp.einsum('bthn,chn->bthc', q[..., :MLA_NOPE], w_uk)
    q_rope = rope(q[..., MLA_NOPE:], pos)
    return q_abs, q_rope, ckv, kr

def mla_out(ctx, w_uv, w_o):
    bsz, t = ctx.shape[:2]
    o = jnp.einsum('bthc,chv->bthv', ctx, w_uv).reshape(bsz, t, MLA_HEADS * MLA_V)
    return o @ w_o

def mla_prompt_attend(q_abs, q_rope, ckv, kr):
    bsz, t = q_abs.shape[:2]
    nb = t // Q_BLOCK
    qa = q_abs.reshape(bsz, nb, Q_BLOCK, MLA_HEADS, MLA_KV_RANK).swapaxes(0, 1)
    qr = q_rope.reshape(bsz, nb, Q_BLOCK, MLA_HEADS, MLA_ROPE).swapaxes(0, 1)
    key_pos = jnp.arange(t)

    def block(args):
        qa_b, qr_b, start = args
        s = (jnp.einsum('bqhc,bkc->bhqk', qa_b, ckv)
             + jnp.einsum('bqhr,bkr->bhqk', qr_b, kr)).astype(jnp.float32) * MLA_SCALE
        q_pos = start + jnp.arange(Q_BLOCK)
        s = jnp.where(key_pos[None, :] <= q_pos[:, None], s, -jnp.inf)
        p = jax.nn.softmax(s, -1).astype(ckv.dtype)
        return jnp.einsum('bhqk,bkc->bqhc', p, ckv)

    ctx = lax.map(block, (qa, qr, jnp.arange(nb) * Q_BLOCK))
    return ctx.swapaxes(0, 1).reshape(bsz, t, MLA_HEADS, MLA_KV_RANK)

def mla_sample_attend(q_abs, q_rope, ckv_new, kr_new, ckv_past, kr_past):
    t = q_abs.shape[1]
    p_len = ckv_past.shape[1]
    s_past = (jnp.einsum('bqhc,bkc->bhqk', q_abs, ckv_past)
              + jnp.einsum('bqhr,bkr->bhqk', q_rope, kr_past)).astype(jnp.float32) * MLA_SCALE
    s_new = (jnp.einsum('bqhc,bkc->bhqk', q_abs, ckv_new)
             + jnp.einsum('bqhr,bkr->bhqk', q_rope, kr_new)).astype(jnp.float32) * MLA_SCALE
    s_new = jnp.where(jnp.tril(jnp.ones((t, t), dtype=bool)), s_new, -jnp.inf)
    p = jax.nn.softmax(jnp.concatenate([s_past, s_new], -1), -1).astype(ckv_new.dtype)
    return (jnp.einsum('bhqk,bkc->bqhc', p[..., :p_len], ckv_past)
            + jnp.einsum('bhqk,bkc->bqhc', p[..., p_len:], ckv_new))

def setup_inputs(seed: int = 0) -> dict:
    key = jax.random.key(seed)
    ks = iter(jax.random.split(key, 48))
    f32 = jnp.float32

    def nrm(shape, scale):
        return jax.random.normal(next(ks), shape, f32) * scale

    def gain(shape):
        return 1.0 + nrm(shape, 0.01)

    n_pages = PAST_LEN // PAGE_SIZE
    n_pool = (DEC_BATCH * n_pages * 5) // 4
    d = D_MODEL
    inputs = {}
    inputs['x_prompt'] = nrm((BATCH, SEQ, d), 1.0)
    inputs['x_sample'] = nrm((DEC_BATCH, DEC_SEQ, d), 1.0)
    inputs['cache_ckv'] = nrm((N_MLA_LAYERS, n_pool, PAGE_SIZE, MLA_KV_RANK), 1.0)
    inputs['cache_krope'] = nrm((N_MLA_LAYERS, n_pool, PAGE_SIZE, MLA_ROPE), 1.0)
    inputs['state_conv'] = nrm((N_CONV_LAYERS, DEC_BATCH, CONV_WIDTH - 1, d), 0.5)
    perm = jax.random.permutation(next(ks), n_pool)[:DEC_BATCH * n_pages]
    inputs['page_table'] = perm.reshape(DEC_BATCH, n_pages).astype(jnp.int32)
    inputs['c_prompt'] = nrm((BATCH, d), 1.0)
    inputs['c_sample'] = nrm((DEC_BATCH, d), 1.0)
    inputs['ada_w'] = nrm((DEPTH, d, 6 * d), d ** -0.5)
    inputs['ada_b'] = nrm((DEPTH, 6 * d), 0.01)
    inputs['ln_mix_g'] = gain((DEPTH, d))
    inputs['ln_mix_b'] = nrm((DEPTH, d), 0.01)
    inputs['ln_ffn_g'] = gain((DEPTH, d))
    inputs['ln_ffn_b'] = nrm((DEPTH, d), 0.01)
    inputs['ffn_w_gate'] = nrm((DEPTH, d, FFN_DIM), d ** -0.5)
    inputs['ffn_w_up'] = nrm((DEPTH, d, FFN_DIM), d ** -0.5 * BETA)
    inputs['ffn_w_down'] = nrm((DEPTH, FFN_DIM, d), FFN_DIM ** -0.5 * BETA)
    inputs['gmlp_w_in'] = nrm((N_GMLP_LAYERS, d, 2 * GMLP_DIM), d ** -0.5)
    inputs['gmlp_ln_g'] = gain((N_GMLP_LAYERS, GMLP_DIM))
    inputs['gmlp_ln_b'] = nrm((N_GMLP_LAYERS, GMLP_DIM), 0.01)
    inputs['gmlp_w_s'] = nrm((N_GMLP_LAYERS, GMLP_GROUPS, GMLP_CHUNK, GMLP_CHUNK), GMLP_CHUNK ** -0.5)
    inputs['gmlp_b_s'] = 1.0 + nrm((N_GMLP_LAYERS, GMLP_GROUPS, GMLP_CHUNK), 0.1)
    inputs['gmlp_w_out'] = nrm((N_GMLP_LAYERS, GMLP_DIM, d), GMLP_DIM ** -0.5 * BETA)
    inputs['conv_w_pw1'] = nrm((N_CONV_LAYERS, d, 2 * d), d ** -0.5)
    inputs['conv_b_pw1'] = nrm((N_CONV_LAYERS, 2 * d), 0.01)
    inputs['conv_w_dw'] = nrm((N_CONV_LAYERS, CONV_WIDTH, d), CONV_WIDTH ** -0.5)
    inputs['conv_b_dw'] = nrm((N_CONV_LAYERS, d), 0.01)
    inputs['conv_ln_g'] = gain((N_CONV_LAYERS, d))
    inputs['conv_ln_b'] = nrm((N_CONV_LAYERS, d), 0.01)
    inputs['conv_w_pw2'] = nrm((N_CONV_LAYERS, d, d), d ** -0.5 * BETA)
    inputs['conv_b_pw2'] = nrm((N_CONV_LAYERS, d), 0.01)
    inputs['mla_w_down'] = nrm((N_MLA_LAYERS, d, MLA_Q_RANK + MLA_KV_RANK + MLA_ROPE), d ** -0.5)
    inputs['mla_g_q'] = gain((N_MLA_LAYERS, MLA_Q_RANK))
    inputs['mla_g_kv'] = gain((N_MLA_LAYERS, MLA_KV_RANK))
    inputs['mla_w_uq'] = nrm((N_MLA_LAYERS, MLA_Q_RANK, MLA_HEADS * (MLA_NOPE + MLA_ROPE)), MLA_Q_RANK ** -0.5)
    inputs['mla_w_uk'] = nrm((N_MLA_LAYERS, MLA_KV_RANK, MLA_HEADS, MLA_NOPE), MLA_KV_RANK ** -0.5)
    inputs['mla_w_uv'] = nrm((N_MLA_LAYERS, MLA_KV_RANK, MLA_HEADS, MLA_V), MLA_KV_RANK ** -0.5 * BETA)
    inputs['mla_w_o'] = nrm((N_MLA_LAYERS, MLA_HEADS * MLA_V, d), (MLA_HEADS * MLA_V) ** -0.5 * BETA)
    return inputs

def reference(x_prompt, x_sample, cache_ckv, cache_krope, state_conv, page_table, c_prompt, c_sample,
              ada_w, ada_b, ln_mix_g, ln_mix_b, ln_ffn_g, ln_ffn_b, ffn_w_gate, ffn_w_up, ffn_w_down,
              gmlp_w_in, gmlp_ln_g, gmlp_ln_b, gmlp_w_s, gmlp_b_s, gmlp_w_out,
              conv_w_pw1, conv_b_pw1, conv_w_dw, conv_b_dw, conv_ln_g, conv_ln_b, conv_w_pw2, conv_b_pw2,
              mla_w_down, mla_g_q, mla_g_kv, mla_w_uq, mla_w_uk, mla_w_uv, mla_w_o):
    dec_b = x_sample.shape[0]
    past_len = page_table.shape[1] * cache_ckv.shape[2]
    pos_p = jnp.arange(x_prompt.shape[1])
    pos_s = past_len + jnp.arange(x_sample.shape[1])
    xp, xs = x_prompt, x_sample
    ckv_p_rows, kr_p_rows, ckv_s_rows, kr_s_rows = [], [], [], []
    conv_p_states, conv_s_states, gmlp_v_rows = [], [], []
    for i in range(DEPTH):
        kind, j = i % N_MIXERS, i // N_MIXERS
        sh1p, sc1p, g1p, sh2p, sc2p, g2p = adaln(c_prompt, ada_w[i], ada_b[i])
        sh1s, sc1s, g1s, sh2s, sc2s, g2s = adaln(c_sample, ada_w[i], ada_b[i])
        hp = xp * (1 + sc1p) + sh1p
        hs = xs * (1 + sc1s) + sh1s
        if kind == 0:
            op, _ = gmlp_mixer(hp, gmlp_w_in[j], gmlp_ln_g[j], gmlp_ln_b[j], gmlp_w_s[j], gmlp_b_s[j], gmlp_w_out[j])
            os_, v_s = gmlp_mixer(hs, gmlp_w_in[j], gmlp_ln_g[j], gmlp_ln_b[j], gmlp_w_s[j], gmlp_b_s[j], gmlp_w_out[j])
            gmlp_v_rows.append(v_s)
        elif kind == 1:
            ctx0 = jnp.zeros((xp.shape[0], CONV_WIDTH - 1, D_MODEL), xp.dtype)
            op, st_p = conv_module(hp, ctx0, conv_w_pw1[j], conv_b_pw1[j], conv_w_dw[j], conv_b_dw[j],
                                   conv_ln_g[j], conv_ln_b[j], conv_w_pw2[j], conv_b_pw2[j])
            os_, st_s = conv_module(hs, state_conv[j], conv_w_pw1[j], conv_b_pw1[j], conv_w_dw[j], conv_b_dw[j],
                                    conv_ln_g[j], conv_ln_b[j], conv_w_pw2[j], conv_b_pw2[j])
            conv_p_states.append(st_p)
            conv_s_states.append(st_s)
        else:
            qa, qr, ckv, kr = mla_project(hp, pos_p, mla_w_down[j], mla_g_q[j], mla_g_kv[j], mla_w_uq[j], mla_w_uk[j])
            op = mla_out(mla_prompt_attend(qa, qr, ckv, kr), mla_w_uv[j], mla_w_o[j])
            ckv_p_rows.append(ckv)
            kr_p_rows.append(kr)
            qa, qr, ckv, kr = mla_project(hs, pos_s, mla_w_down[j], mla_g_q[j], mla_g_kv[j], mla_w_uq[j], mla_w_uk[j])
            ckv_past = cache_ckv[j, page_table].reshape(dec_b, past_len, MLA_KV_RANK)
            kr_past = cache_krope[j, page_table].reshape(dec_b, past_len, MLA_ROPE)
            os_ = mla_out(mla_sample_attend(qa, qr, ckv, kr, ckv_past, kr_past), mla_w_uv[j], mla_w_o[j])
            ckv_s_rows.append(ckv)
            kr_s_rows.append(kr)
        xp = layer_norm(ALPHA * xp + g1p * op, ln_mix_g[i], ln_mix_b[i])
        xs = layer_norm(ALPHA * xs + g1s * os_, ln_mix_g[i], ln_mix_b[i])
        fp = swiglu_ffn(xp * (1 + sc2p) + sh2p, ffn_w_gate[i], ffn_w_up[i], ffn_w_down[i])
        fs = swiglu_ffn(xs * (1 + sc2s) + sh2s, ffn_w_gate[i], ffn_w_up[i], ffn_w_down[i])
        xp = layer_norm(ALPHA * xp + g2p * fp, ln_ffn_g[i], ln_ffn_b[i])
        xs = layer_norm(ALPHA * xs + g2s * fs, ln_ffn_g[i], ln_ffn_b[i])
    return (xp, xs, jnp.stack(ckv_p_rows), jnp.stack(kr_p_rows), jnp.stack(ckv_s_rows), jnp.stack(kr_s_rows),
            jnp.stack(conv_p_states), jnp.stack(conv_s_states), jnp.stack(gmlp_v_rows))


_drawn_inputs = setup_inputs


def setup_inputs(seed=0):
    import zlib

    import numpy as np

    out = dict(_drawn_inputs(seed))
    spreads = {}
    factors = {'cache_ckv': 8.0,
     'cache_krope': 8.0,
     'ada_b': 4.386,
     'ln_mix_g': 2.873,
     'ln_mix_b': 2.814,
     'ln_ffn_g': 2.961,
     'ln_ffn_b': 2.891,
     'gmlp_ln_g': 20.635,
     'gmlp_ln_b': 21.553,
     'gmlp_b_s': 3.036,
     'conv_b_pw1': 6.842,
     'conv_b_dw': 8.0,
     'conv_ln_g': 45.522,
     'conv_ln_b': 37.802,
     'conv_b_pw2': 8.0,
     'mla_g_q': 8.0,
     'mla_g_kv': 18.168,
     'mla_w_uq': 8.0,
     'mla_w_uk': 8.0}
    for name, (base, spread) in spreads.items():
        noise = np.random.default_rng([zlib.crc32(name.encode()), seed]).standard_normal(out[name].shape)
        drawn = base * np.exp(spread * noise) if base else spread * noise
        out[name] = __import__('jax').numpy.asarray(drawn.astype(out[name].dtype))
    for name, factor in factors.items():
        out[name] = (out[name] * factor).astype(out[name].dtype)
    return out
```

```python
from contextlib import ExitStack, contextmanager

import numpy as np

import concourse.bass as bass
from concourse import mybir

F32 = mybir.dt.float32
F32R = mybir.dt.float32r
I32 = mybir.dt.int32
ACT = mybir.ActivationFunctionType
ALU = mybir.AluOpType
AX = mybir.AxisListType

P = 128
D = 1024
KT = D // P
SEQ = 512
DEC_B, DEC_T = 8, 8
NS = DEC_B * DEC_T
TOK = SEQ + NS
HALF = TOK // 2
HP = SEQ - HALF
TT = 5
DEPTH = 4
NC = 1 + DEC_B
ADA_M = 6 * KT
FFN = 2816
GDIM = 2048
GROUPS = 8
CW = 31
CTX = CW - 1
HEADS, NOPE, ROPE, VD = 8, 128, 64, 128
QR, KVR = 384, 256
DOWN = QR + KVR + ROPE
PAGES, PAGE = 8, 128
PAST = PAGES * PAGE
R = HEADS * DEC_T
ALPHA = (2.0 * DEPTH) ** 0.25
LN_EPS, RMS_EPS = 1e-5, 1e-6
SCALE = (NOPE + ROPE) ** -0.5
NEG = -1e30
UNIT = 1024
RAW, SLOTS, BANKS = 2, 4, 4

C_ADA, C_LN, C_PW1, C_DW, C_CG, C_CB, C_PW2, C_C = 0, 192, 320, 336, 344, 352, 360, 368
C_END = C_C + NC * KT
FULL = CTX + SEQ + DEC_B * (CTX + DEC_T)


class Tally:

    def __init__(self, start=0):
        self.v = start
        self.n = start

    def up(self, k=1):
        self.v = self.v + k
        self.n += k
        return self.v


@contextmanager
def rolled(eng, trips, *steps):
    starts = [(t, s, t.v, t.n) for t, s in steps]
    if trips == 1:
        yield 0
        for t, s, v, n in starts:
            assert t.n == n + s
        return
    with eng.Fori(0, trips) as i:
        for t, s, v, n in starts:
            t.v = i * s + v
        yield i
    for t, s, v, n in starts:
        assert t.n == n + s, (t.n, n, s)
        t.v, t.n = v + trips * s, n + trips * s


N_SETUP = 16
OUTS, VOUTS = 3, 8


def SAMPLE_BANK(b, q):
    return BANKS + (13 * b + 6 + q) % BANKS


def token_tile(t):
    return slice(TOK - P, TOK) if t == TT - 1 else slice(t * P, (t + 1) * P)


def half_cols(h):
    return slice(h * HALF, (h + 1) * HALF)


def trunk(nc, A, O):
    ctx = ExitStack()
    with ctx:
        def sem(name):
            return ctx.enter_context(nc.semaphore(name))

        top = [-(-nc.sbuf_base // 64) * 64]

        def at(name, shape, dt, offset):
            return nc.alloc_sbuf_tensor_at(name, shape, dt, offset=offset)

        def size(shape):
            n = 4
            for s in shape[1:]:
                n *= s
            return -(-n // 64) * 64

        def sb(name, shape, dt=F32):
            t = at(name, shape, dt, top[0])
            top[0] += size(shape)
            return t

        def region(nbytes):
            start = top[0]
            top[0] += nbytes
            return start

        class Place:

            def __init__(self, start, nbytes, tag):
                self.at, self.end, self.tag = start, start + nbytes, tag

            def __call__(self, name, shape, dt=F32):
                t = at(name, shape, dt, self.at)
                self.at += size(shape)
                assert self.at <= self.end, (self.tag, name, self.at - self.end)
                return t

        ident = sb("ident", [P, P])
        ones = sb("ones", [P, P])
        xa = sb("xa", [P, KT, TOK])
        par = sb("par", [P, C_END])
        cs = sb("cs", [P, 2 * DEPTH, KT, NC])
        cb = sb("cb", [P, 2 * DEPTH, KT, NC])
        ag = sb("ag", [P, 2 * DEPTH + 1, KT])
        ab = sb("ab", [P, 2 * DEPTH + 1, KT])
        gate = sb("gate", [P, 2 * DEPTH, KT, NC])
        epsl = sb("epsl", [P, 2])
        smt = sb("smt", [P, NS])
        pt_sb = sb("pt_sb", [1, DEC_B * PAGES], I32)
        w_raw = sb("w_raw", [P, RAW, UNIT])
        w_hi = sb("w_hi", [P, SLOTS, UNIT], F32R)
        w_lo = sb("w_lo", [P, SLOTS, UNIT], F32R)
        HB = 2 * KT * TOK * 4
        h_at = region(HB)
        h_hi = at("h_hi", [P, KT, TOK], F32R, h_at)
        h_lo = at("h_lo", [P, KT, TOK], F32R, h_at + HB // 2)
        a_at = region(HB)
        a_hi = at("a_hi", [P, KT, TOK], F32R, a_at)
        a_lo = at("a_lo", [P, KT, TOK], F32R, a_at + HB // 2)
        LNB = 4 * TOK * 8
        ln_at = region(LNB)
        lp = Place(ln_at, LNB, "ln")
        s_sum = lp("s_sum", [P, TOK])
        s_sq = lp("s_sq", [P, TOK])
        mean = lp("mean", [P, TOK])
        rstd = lp("rstd", [P, TOK])
        sqt = lp("sqt", [P, 2, HALF])
        hf = lp("hf", [P, 2, HALF])
        sg = lp("sg", [P, 2, HALF])
        pr = lp("pr", [P, 2, HALF])
        s_at = top[0]
        SB = nc.sbuf_usable_end - s_at

        sp0 = Place(s_at, SB, "setup")
        x_in = sp0("x_in", [P, TT, D])
        stage = sp0("stage", [P, 4, P])
        mod = sp0("mod", [P, ADA_M, NC])
        cact = sp0("cact", [P, NC, KT])
        ada_row = sp0("ada_row", [NC, 2, 512])
        sp1 = Place(s_at, SB, "gmlp")
        v_sb = sp1("v_sb", [P, TT, GDIM])
        wsT = sp1("wsT", [P, GROUPS, P])
        wssT = sp1("wssT", [P, GROUPS, NS])
        bst = sp1("bst", [P, TT, GROUPS, 6])
        bag = sp1("bag", [P, TT, 2])
        vrs = sp1("vrs", [P, TT])
        gl = Place(ln_at, LNB, "gmlp-ln")
        vn = gl("vn", [P, 2, TT, 256])
        u_sb = gl("u_sb", [P, TOK])
        gbt = gl("gbt", [P, 2, 2, 256])
        bsb = gl("bsb", [P, 2, P])
        ga = Place(a_at, HB, "gmlp-act")
        ws_raw = ga("ws_raw", [P, GROUPS, P])
        wss_raw = ga("wss_raw", [NS, GROUPS, P])
        tril = ga("tril", [P, P])
        sp2 = Place(s_at, SB, "conv")
        full = sp2("full", [P, 2, FULL])
        yc = sp2("yc", [P, KT, TOK])
        stT = sp2("stT", [P, KT, DEC_B * CTX])
        snew = sp2("snew", [P, 2, NS])
        wdT = sp2("wdT", [P, KT, CW])
        st_p = sp2("st_p", [CTX, D])
        st_s = sp2("st_s", [NS, D])
        gbw = sp2("gbw", [P, KT, NC])
        ca = Place(a_at, HB, "conv-act")
        wd_in = ca("wd_in", [CW, D])
        st_in = ca("st_in", [4 * CTX, 2, D])
        sp3 = Place(s_at, SB, "mla")
        qaT = sp3("qaT", [P, 2, HEADS, TOK])
        qr_at = sp3.at
        qrT = sp3("qrT", [P, HEADS // 2, TOK])
        uv = at("uv", [P, 2, D], F32, qr_at)
        qas = sp3("qas", [P, 2, DEC_B, HEADS, DEC_T])
        ml = Place(ln_at, LNB, "mla-ln")
        ckv = ml("ckv", [P, TT, KVR])
        ckvT = ml("ckvT", [P, 2, TOK])
        krT = ml("krT", [P, TOK])
        kr2 = ml("kr2", [P, TT, 2, ROPE])
        qrs = ml("qrs", [ROPE, DEC_B, HEADS, DEC_T])
        mh = Place(h_at, HB, "mla-h")
        ql_hi = mh("ql_hi", [P, 3, TOK], F32R)
        ql_lo = mh("ql_lo", [P, 3, TOK], F32R)
        ukT = mh("ukT", [P, HEADS, KVR])
        qn = mh("qn", [P, 2, TOK])
        rt = mh("rt", [P, 2, HEADS * ROPE // 2])
        ms = Place(h_at, HB, "mla-h2")
        pg = ms("pg", [P, PAGES, KVR])
        pgr = ms("pgr", [P, PAGES, ROPE])
        pgT = ms("pgT", [P, 2, PAST])
        pgrT = ms("pgrT", [ROPE, PAST])
        pe_at = ms.at
        pexp = ms("pexp", [P, 2, 512])
        pT = ms("pT", [P, 2, 4, P])
        mq = Place(pe_at, 8192, "mla-h3")
        sp_ = mq("sp_", [HEADS * DEC_T, PAST + P])
        spT = mq("spT", [P, PAGES + 1, HEADS * DEC_T])
        scx = at("scx", [HEADS * DEC_T, KVR], F32, mq.at)
        ma = Place(a_at, HB, "mla-act")
        dtok = ma("dtok", [P, TT, DOWN])
        qrt = ma("qrt", [P, TT, HEADS * ROPE])
        ukr = ma("ukr", [P, 2, D])
        rtab = ma("rtab", [P, TT, ROPE])
        gqk = ma("gqk", [P, QR + KVR])
        ssq = ma("ssq", [P, TT, 2])
        mb = Place(a_at, HB, "mla-act2")
        cmask = mb("cmask", [P, P])
        smask = mb("smask", [HEADS * DEC_T, DEC_B, P])
        att = mb("att", [P, 2, 8])
        satt = mb("satt", [R, 8])
        yo = at("yo", [P, 2, D], F32, s_at)

        pb = ctx.enter_context(nc.psum_tensor("pb", [P, 8, 512], F32))

        const_in = sem("const_in")
        const_made = sem("const_made")
        raw_full = [sem(f"raw_full{i}") for i in range(RAW)]
        ada_used = sem("ada_used")
        act_c = sem("act_c")
        split_full = sem("split_full")
        split_free = sem("split_free")
        acc_ready = sem("acc_ready")
        acc_free = sem("acc_free")
        aux_ready = sem("aux_ready")
        aux_free = sem("aux_free")
        coef_ready = sem("coef_ready")
        n_ready = sem("n_ready")
        hf_ready = sem("hf_ready")
        h_ready = sem("h_ready")
        xa_ready = sem("xa_ready")
        a_ready = sem("a_ready")
        sq_ready = sem("sq_ready")
        q_done = sem("q_done")
        yc_ready = sem("yc_ready")
        var_ready = sem("var_ready")
        std_ready = sem("std_ready")
        sg_ready = sem("sg_ready")
        v_ready = sem("v_ready")
        ws_in = sem("ws_in")
        ws_zero = sem("ws_zero")
        ws_ready = sem("ws_ready")
        gb_full = [sem(f"gb_full{i}") for i in range(2)]
        vn_ready = sem("vn_ready")
        vo_done = [sem(f"vo_done{i}") for i in range(2)]
        st_in_full = sem("st_in_full")
        full_ready = sem("full_ready")
        st_ready = sem("st_ready")
        d_ready = sem("d_ready")
        ssq_ready = sem("ssq_ready")
        mla_in = sem("mla_in")
        kv_ready = sem("kv_ready")
        kv_out = sem("kv_out")
        lat_ready = sem("lat_ready")
        qr_ready = sem("qr_ready")
        sc_ready = sem("sc_ready")
        nm_ready = sem("nm_ready")
        sc_free = sem("sc_free")
        p_ready = sem("p_ready")
        pt_ready = sem("pt_ready")
        pt_copied = sem("pt_copied")
        mask_in = sem("mask_in")
        pt_in = sem("pt_in")
        pg_full = sem("pg_full")
        pg_used = sem("pg_used")
        se_ready = sem("se_ready")
        uv_full = sem("uv_full")
        yo_ready = sem("yo_ready")
        y_out = [sem(f"y_out{i}") for i in range(2)]
        pool_passed, pe_passed, act_passed = [sem(n + "_passed") for n in ("pool", "pe", "act")]
        out_done = sem("out_done")

        def settle(eng, passed):
            eng.sem_inc(passed, 1)

        def one(t, m, cols=slice(None)):
            if isinstance(m, int):
                return t[:, m, cols]
            return t[:, bass.ds(m, 1), cols].rearrange("p a n -> p (a n)")

        def per_row(t, e, m):
            r = one(t[:, e, :, :], m)
            return r[:, 0:1], r[:, 1:NC].unsqueeze(2).to_broadcast([P, DEC_B, DEC_T])

        def bt(ap):
            return ap.rearrange("p (b t) -> p b t", b=DEC_B)

        def full_s(ap):
            return ap[:, CTX + SEQ:].rearrange("p (b t) -> p b t", b=DEC_B)

        def one1(t, m, off):
            return t[:, off + m:off + m + 1] if isinstance(m, int) else t[:, bass.ds(m + off, 1)]

        def wcols(w, k0, k1, c0, n):
            return w[k0 * P:k1 * P, bass.ds(c0, n)].rearrange("(k p) n -> p k n", p=P)

        GU = ((0, 8), (8, 8), (16, 6))

        def ffn_units(l):
            for first, count in GU:
                yield count // 2, lambda i, first=first: [
                    [wcols(w[l], 0, KT, (i * 2 + (first + mm)) * P, P)]
                    for mm in range(2) for w in (A["ffn_w_gate"], A["ffn_w_up"])]
                yield 2, lambda i, first=first, count=count: [
                    [wcols(A["ffn_w_down"][l], first, first + count, (i * 4 + mm) * P, P)] for mm in range(4)]

        def gmlp_units(j):
            w_in, w_out = A["gmlp_w_in"][j], A["gmlp_w_out"][j]
            yield 2, lambda i: [[wcols(w_in, 4 * kh, 4 * kh + 4, (i * 4 + gg) * 256 + GDIM, 256)]
                                for gg in range(4) for kh in range(2)]
            for ph in range(2):
                yield 2, lambda i, ph=ph: [[wcols(w_in, 0, KT, (i * 4 + (8 * ph + mm)) * P, P)] for mm in range(4)]
                yield 2, lambda i, ph=ph: [[wcols(w_out, 8 * ph, 8 * ph + 8, (i * 4 + mm) * P, P)] for mm in range(4)]

        def conv_units(j):
            yield 4, lambda i: [[wcols(A["conv_w_pw1"][j], 0, KT, (i * 2 + (mm + part * KT)) * P, P)]
                                for mm in range(2) for part in range(2)]
            yield 2, lambda i: [[wcols(A["conv_w_pw2"][j], 0, KT, (i * 4 + mm) * P, P)] for mm in range(4)]

        DCH = ((0, 256), (256, 256), (512, 192))

        def mla_units(j):
            wd, wq = A["mla_w_down"][j], A["mla_w_uq"][j]
            yield 1, lambda i: [[wcols(wd, 4 * kh, 4 * kh + 4, c0, n)] for c0, n in DCH for kh in range(2)]
            wr = wq.rearrange("(k p) (h n) -> k p h n", p=P, h=HEADS)
            yield 1, lambda i: [[wr[k, :, 4 * c:4 * c + 4, NOPE:] for k in range(3)] for c in range(2)]
            yield 1, lambda i: [[wcols(wq, 0, 3, h * (NOPE + ROPE), NOPE)] for h in range(HEADS)]
            yield 2, lambda i: [[wcols(A["mla_w_o"][j], 0, KT, (i * 4 + mm) * P, P)] for mm in range(4)]

        block = ctx.enter_context(nc.Block())

        @block.sync
        def _(sp):
            n_setup = 0
            ada_b = A["ada_b"].rearrange("l (m c) -> (l m) c", c=P)
            loads = [
                (ident[:], A["c_ident"]),
                (stage[:, 0, :], ada_b[0:P]),
                (stage[0:DEPTH * ADA_M - P, 1, :], ada_b[P:]),
            ]
            for n, name in enumerate(("ln_mix_g", "ln_mix_b", "ln_ffn_g", "ln_ffn_b")):
                loads.append((stage[32 * n:32 * n + 32, 2, :], A[name].rearrange("l (m c) -> (l m) c", c=P)))
            row = 0
            for name in ("conv_b_pw1", "conv_b_dw", "conv_ln_g", "conv_ln_b", "conv_b_pw2", "c_prompt", "c_sample"):
                src = A[name].rearrange("l (m c) -> (l m) c", c=P)
                loads.append((stage[row:row + src.shape[0], 3, :], src))
                row += src.shape[0]
            loads.append((x_in[:, 0:4, :], A["x_prompt"][0].rearrange("(t p) d -> p t d", p=P)))
            loads.append((x_in[0:NS, 4, :], A["x_sample"].rearrange("b t d -> (b t) d")))
            for dst, src in loads:
                sp.dma_start(dst, src).then_inc(const_in, 16)
            units = Tally()
            arrived = [Tally(), Tally()]
            ada_u = Tally()
            for l in range(DEPTH):
                with rolled(sp, 6, (ada_u, 8), (arrived[0], 64), (arrived[1], 64)) as i:
                    for c in range(2):
                        for q in range(4):
                            sp.wait_ge(ada_used, ada_u.v + 1)
                            s = ada_u.n % RAW
                            sp.dma_start(w_raw[:, s, :].rearrange("p (k n) -> p k n", k=2),
                                         wcols(A["ada_w"][l], 2 * q, 2 * q + 2, i * 1024 + c * 512, 512)
                                         ).then_inc(raw_full[s], 16)
                            arrived[s].up(16)
                            ada_u.up()
            sp.wait_ge(ada_used, ada_u.v + RAW)

            def stream(segments, before_unit=None, steps=()):
                for trips, units_of in segments:
                    n = len(units_of(0))
                    per = [0, 0]
                    for u, srcs in enumerate(units_of(0)):
                        per[(units.n + u) % RAW] += 16 * len(srcs)
                    with rolled(sp, trips, (units, n), (arrived[0], per[0]), (arrived[1], per[1]), *steps) as i:
                        for u, srcs in enumerate(units_of(i)):
                            if before_unit:
                                before_unit(i, u)
                            sp.wait_ge(split_full, units.v + 1)
                            s = units.n % RAW
                            at_ = 0
                            for src in srcs:
                                words = src.shape[1] * src.shape[2]
                                sp.dma_start(w_raw[:, s, at_:at_ + words].rearrange(
                                    "p (k n) -> p k n", k=src.shape[1]), src).then_inc(raw_full[s], 16)
                                at_ += words
                            arrived[s].up(16 * len(srcs))
                            units.up()

            gb_n = [0, 0]
            a_n = Tally()
            for l in range(DEPTH):
                j, t = l // 3, 2 * l
                if l % 3 == 0:
                    segs = list(gmlp_units(j))
                    if l:
                        sp.wait_ge(h_ready, 16 * t + 9)
                    sp.wait_ge(ws_zero, j + 1)
                    ws = A["gmlp_w_s"][j]
                    sp.dma_start(ws_raw[:], ws.rearrange("g t s -> t g s")).then_inc(ws_in, 16)
                    sp.dma_start(tril[:], A["c_tril"]).then_inc(ws_in, 16)
                    for b in range(DEC_B):
                        sp.dma_start(wss_raw[8 * b:8 * b + 8, :, NS + 8 * b:NS + 8 * b + 8],
                                     ws[:, 0:8, 0:8].rearrange("g t s -> t g s")).then_inc(ws_in, 16)
                    stream(segs[0:1])
                    sp.wait_ge(h_ready, 16 * t + 16)
                    for ph in range(2):
                        def rows(i, u, ph=ph):
                            if u % 2 == 0:
                                par_ = u // 2
                                sp.wait_ge(a_ready, 8 + a_n.v - 4)
                                g = i * 2 + (4 * ph + par_)
                                for n, name in enumerate(("gmlp_ln_g", "gmlp_ln_b")):
                                    sp.dma_start(gbt[:, par_, n, :], A[name][j, bass.ds(g * 256, 256)]
                                                 .partition_broadcast(P)).then_inc(gb_full[par_], 16)
                                sp.dma_start(bsb[:, par_, :], A["gmlp_b_s"][j, bass.ds(g, 1), :]
                                             .broadcast_to([P, P])).then_inc(gb_full[par_], 16)
                                a_n.up(4)
                        stream(segs[1 + 2 * ph:2 + 2 * ph], rows, ((a_n, 8),))
                        stream(segs[2 + 2 * ph:3 + 2 * ph])
                elif l % 3 == 1:
                    sp.wait_ge(h_ready, 16 * t + 9)
                    st = A["state_conv"][j].rearrange("b r d -> (b r) d")
                    for n in range(2):
                        sp.dma_start(st_in[:, n, :], st[n * 4 * CTX:(n + 1) * 4 * CTX]).then_inc(st_in_full, 16)
                    sp.dma_start(wd_in[:], A["conv_w_dw"][j]).then_inc(st_in_full, 16)
                    sp.dma_start(O["new_conv_sample"][j, :, 0:CTX - DEC_T, :],
                                 A["state_conv"][j, :, DEC_T:, :]).then_inc(out_done, 16)
                    stream(conv_units(j))
                    a_n.up(16)
                else:
                    segs = list(mla_units(j))
                    sp.wait_ge(h_ready, 16 * t + 9)
                    sp.dma_start(rtab[:], A["c_rope"]).then_inc(mla_in, 16)
                    sp.dma_start(gqk[:, 0:QR], A["mla_g_q"][j].partition_broadcast(P)).then_inc(mla_in, 16)
                    sp.dma_start(gqk[:, QR:], A["mla_g_kv"][j].partition_broadcast(P)).then_inc(mla_in, 16)
                    sp.dma_start(ukr[:], A["mla_w_uk"][j].rearrange("(c p) h n -> p c (h n)", p=P)
                                 ).then_inc(mla_in, 16)
                    sp.dma_start(pt_sb[:], A["page_table"].rearrange("b g -> (b g)").unsqueeze(0)
                                 ).then_inc(pt_in, 16)
                    stream(segs[0:3])
                    sp.wait_ge(pt_in, 16)
                    sp.wait_ge(sc_ready, 1)
                    sp.dma_start(cmask[:], A["c_causal"]).then_inc(mask_in, 16)
                    sp.dma_start(smask[:], A["c_smask"]).then_inc(mask_in, 16)
                    for b in range(DEC_B):
                        if b:
                            sp.wait_ge(pg_used, b)
                        for g in range(PAGES):
                            page = sp.value_load(pt_sb[0:1, b * PAGES + g:b * PAGES + g + 1],
                                                 min_val=0, max_val=A["cache_ckv"].shape[1] - 1)
                            sp.dma_start(pg[:, g, :].unsqueeze(1), A["cache_ckv"][j, bass.ds(page, 1)]
                                         .rearrange("a p c -> p a c")).then_inc(pg_full, 16)
                            sp.dma_start(pgr[:, g, :].unsqueeze(1), A["cache_krope"][j, bass.ds(page, 1)]
                                         .rearrange("a p c -> p a c")).then_inc(pg_full, 16)
                    sp.wait_ge(pg_used, DEC_B)
                    sp.dma_start(uv[:], A["mla_w_uv"][j].rearrange("(c p) h v -> p c (h v)", p=P)
                                 ).then_inc(uv_full, 16)
                    stream(segs[3:4])
                    a_n.up(16)
                stream(ffn_units(l))
                a_n.up(2 * FFN // P)
            for tt in range(TT):
                sp.wait_ge(yo_ready, tt + 1)
                dst = (O["y_prompt"][0, tt * P:(tt + 1) * P, :] if tt < 4
                       else O["y_sample"].rearrange("b t d -> (b t) d"))
                sp.dma_start(dst, yo[0:dst.shape[0], tt % 2, :]).then_inc(y_out[tt % 2], 16)
            sp.wait_ge(y_out[0], 48)
            sp.wait_ge(y_out[1], 32)
            sp.wait_ge(out_done, OUTS * 16)
            for n in range(2):
                sp.wait_ge(vo_done[n], VOUTS * 16 + 16)
            sp.wait_ge(kv_out, 64)

        @block.gpsimd
        def _(pool):
            pool.sem_inc(split_full, RAW)
            units = Tally()
            arrived = [Tally(16 * DEPTH * 24), Tally(16 * DEPTH * 24)]
            for l in range(DEPTH):
                segs = (gmlp_units, conv_units, mla_units)[l % 3](l // 3)
                for trips, units_of in [*segs, *ffn_units(l)]:
                    n = len(units_of(0))
                    per = [0, 0]
                    for u, srcs in enumerate(units_of(0)):
                        per[(units.n + u) % RAW] += 16 * len(srcs)
                    words = [sum(s.shape[1] * s.shape[2] for s in srcs) for srcs in units_of(0)]
                    parts = [len(srcs) for srcs in units_of(0)]
                    with rolled(pool, trips, (units, n), (arrived[0], per[0]), (arrived[1], per[1])):
                        for w, k in zip(words, parts):
                            s, r = units.n % SLOTS, units.n % RAW
                            arrived[r].up(16 * k)
                            pool.wait_ge(raw_full[r], arrived[r].v)
                            pool.wait_ge(split_free, units.v + 1)
                            settle(pool, pool_passed)
                            nc.gpsimd.tensor_scalar(w_hi[:, s, 0:w], w_raw[:, r, 0:w], 1.0, 1.0, ALU.mult, ALU.mult)
                            pool.drain()
                            nc.gpsimd.tensor_tensor(w_lo[:, s, 0:w], w_raw[:, r, 0:w],
                                                    w_hi[:, s, 0:w].bitcast(F32), ALU.subtract
                                                    ).then_inc(split_full, 1)
                            units.up()

        @block.tensor
        def _(pe):
            pe.sem_inc(ada_used, RAW)
            pe.sem_inc(split_free, SLOTS)
            U, G, X, AR = Tally(), Tally(), Tally(), Tally()

            def take_units(k):
                pe.wait_ge(split_full, U.v + k + RAW)
                slots = [(U.n + n) % SLOTS for n in range(k)]
                U.up(k)
                return slots

            def mm(out, lhsT, rhs, start, stop):
                return nc.tensor.matmul(out, lhsT, rhs, start=start, stop=stop)

            def flush(k):
                pe.drain().then_inc(split_free, k)

            def acc_bank():
                pe.wait_ge(acc_free, G.v + 1)
                return G.n % BANKS

            def aux_bank():
                pe.wait_ge(aux_free, X.v + 1)
                return BANKS + X.n % BANKS

            def product(out, ks, w_at, m_hi, m_lo, w_moves=False):
                n = len(ks)
                for q, k in enumerate(ks):
                    s, cols = w_at(k)
                    wh, wl = w_hi[:, s, cols], w_lo[:, s, cols]
                    ah, al = m_hi(k), m_lo(k)
                    for e, (w, a) in enumerate(((wh, ah), (wh, al), (wl, ah))):
                        lhsT, rhs = (a, w) if w_moves else (w, a)
                        last = mm(out, lhsT, rhs, q == 0 and e == 0, q == n - 1 and e == 2)
                return last

            def half_product(slot, kt, h, act, waits=None):
                b = acc_bank()
                hi, lo = act
                if waits is not None:
                    for k in range(kt):
                        pe.wait_ge(h_ready, waits + 8 * h + k + 1)
                        for e, (w, a) in enumerate(((w_hi, hi), (w_hi, lo), (w_lo, hi))):
                            last = mm(pb[:, b, 0:HALF], w[:, slot, k * P:(k + 1) * P], a[:, k, half_cols(h)],
                                      k == 0 and e == 0, k == kt - 1 and e == 2)
                else:
                    last = product(pb[:, b, 0:HALF], range(kt), lambda k: (slot, slice(k * P, (k + 1) * P)),
                                   lambda k: hi[:, k, half_cols(h)], lambda k: lo[:, k, half_cols(h)])
                last.then_inc(acc_ready, 1)
                G.up()

            def transposes(parts):
                b = aux_bank()
                settle(pe, pe_passed)
                for n, (c0, src) in enumerate(parts):
                    rows, cols = src.shape
                    last = nc.tensor.transpose(pb[0:cols, b, c0:c0 + rows], src, ident[0:rows, 0:rows])
                last.then_inc(aux_ready, 1)
                X.up()

            def down(kt):
                with rolled(pe, 2, (U, 4), (G, 8)):
                    for mm_ in range(4):
                        (s,) = take_units(1)
                        for h in range(2):
                            pe.wait_ge(a_ready, 8 + AR.v - 1 + h)
                            half_product(s, kt, h, (a_hi, a_lo))
                        flush(1)

            def stats():
                for h in range(2):
                    pe.wait_ge(q_done, 2 + QD.v + 15 + h)
                    for src in (s_sum, s_sq):
                        b = aux_bank()
                        mm(pb[:, b, 0:HALF], ones[:], src[:, half_cols(h)], True, True).then_inc(aux_ready, 1)
                        X.up()
                QD.up(16)

            QD = Tally()

            def gate_up(count, wait_h):
                with rolled(pe, count // 2, (U, 4), (G, 8)):
                    for m in range(2):
                        s_a, s_b = take_units(2)
                        for h in range(2):
                            for s in (s_a, s_b):
                                half_product(s, KT, h, (h_hi, h_lo), wait_h)
                        flush(2)

            pe.wait_ge(const_in, 16 * N_SETUP)
            pe.wait_ge(const_made, 1)
            for n, rows in enumerate((P, DEPTH * ADA_M - P, P, C_END - C_PW1)):
                transposes([(0, stage[0:rows, n, :])])
            for tt in range(TT):
                rows = P if tt < 4 else NS
                for q in range(2):
                    transposes([(i * P, x_in[0:rows, tt, (4 * q + i) * P:(4 * q + i + 1) * P]) for i in range(4)])
            pe.wait_ge(act_c, 1)
            ada_u = Tally()
            arrived = [Tally(), Tally()]
            for l in range(DEPTH):
                with rolled(pe, 6, (ada_u, 8), (X, 4), (arrived[0], 64), (arrived[1], 64)):
                    for c in range(2):
                        b = aux_bank()
                        for q in range(4):
                            s = ada_u.n % RAW
                            arrived[s].up(16)
                            pe.wait_ge(raw_full[s], arrived[s].v)
                            for k in range(2):
                                last = mm(pb[0:NC, b, :], cact[:, :, 2 * q + k],
                                          w_raw[:, s, k * 512:(k + 1) * 512], q == 0 and k == 0, q == 3 and k == 1)
                            if q < 3:
                                last.then_inc(ada_used, 1)
                            ada_u.up()
                        last.then_inc(aux_ready, 1)
                        pe.drain().then_inc(ada_used, 1)
                        X.up()
                        pe.wait_ge(aux_free, X.v + BANKS)
                        b = aux_bank()
                        settle(pe, pe_passed)
                        for i in range(4):
                            last = nc.tensor.transpose(pb[:, b, i * NC:(i + 1) * NC], ada_row[:, c, i * P:(i + 1) * P],
                                                       ident[0:NC, 0:NC])
                        last.then_inc(aux_ready, 1)
                        X.up()

            def gmlp(l):
                t = 2 * l
                with rolled(pe, 2, (U, 8), (G, 20)):
                    for gg in range(4):
                        slots = take_units(2)
                        for tt in range(TT):
                            pe.wait_ge(h_ready, 16 * t + (8 if tt < 2 else 16))
                            b = acc_bank()
                            product(pb[:, b, 0:256], range(KT),
                                    lambda k: (slots[k // 4], slice(k % 4 * 256, k % 4 * 256 + 256)),
                                    lambda k: h_hi[:, k, token_tile(tt)], lambda k: h_lo[:, k, token_tile(tt)],
                                    w_moves=True).then_inc(acc_ready, 1)
                            G.up()
                        flush(2)
                pe.wait_ge(ws_ready, l // 3 + 1)
                for q in range(2):
                    transposes([(i * P, ws_raw[:, 4 * q + i, :]) for i in range(4)])
                transposes([(g * NS, wss_raw[:, g, :]) for g in range(GROUPS)])
                for ph in range(2):
                    with rolled(pe, 2, (U, 4), (G, 8), (X, 8), (VN, 2)) as i:
                        for gg in range(2):
                            g = i * 2 + (4 * ph + gg)
                            VN.up()
                            for mt in range(2):
                                (s,) = take_units(1)
                                for h in range(2):
                                    half_product(s, KT, h, (h_hi, h_lo))
                                flush(1)
                                pe.wait_ge(vn_ready, VN.v)
                                b = aux_bank()
                                for tt in range(4):
                                    last = mm(pb[:, b, tt * P:(tt + 1) * P], vn[:, gg, tt, mt * P:(mt + 1) * P],
                                              one(wsT, g), True, True)
                                last.then_inc(aux_ready, 1)
                                X.up()
                                b = aux_bank()
                                mm(pb[:, b, 0:NS], vn[:, gg, 4, mt * P:(mt + 1) * P], one(wssT, g),
                                   True, True).then_inc(aux_ready, 1)
                                X.up()
                    AR.up(16)
                    down(KT)
                stats()

            VN = Tally()

            def conv(l):
                t = 2 * l
                pe.wait_ge(st_in_full, 48)
                transposes([(k * CW, wd_in[:, k * P:(k + 1) * P]) for k in range(KT)])
                for k in range(KT):
                    transposes([(n * 4 * CTX, st_in[:, n, k * P:(k + 1) * P]) for n in range(2)])
                FR = Tally()
                with rolled(pe, 4, (U, 4), (G, 8), (X, 4), (FR, 2)):
                    for m in range(2):
                        s_a, s_b = take_units(2)
                        for h in range(2):
                            for s in (s_a, s_b):
                                half_product(s, KT, h, (h_hi, h_lo), 16 * t)
                        flush(2)
                    for m in range(2):
                        pe.wait_ge(full_ready, FR.up())
                        transposes([(0, full[:, m, SEQ:SEQ + CTX])])
                        transposes([(0, snew[:, m, :])])
                stats()
                AR.up(16)
                down(KT)
                stats()

            def tok_major(chunks, kts, hi, lo, waits):
                for slots_of, n, nslots in chunks:
                    slots = take_units(nslots)
                    for tt in range(TT):
                        if waits is not None:
                            pe.wait_ge(h_ready, waits + (8 if tt < 2 else 16))
                        b = acc_bank()
                        product(pb[:, b, 0:n], range(kts),
                                lambda k: (slots[slots_of(k)[0]], slice(slots_of(k)[1] * n, (slots_of(k)[1] + 1) * n)),
                                lambda k: hi[:, k, token_tile(tt)], lambda k: lo[:, k, token_tile(tt)],
                                w_moves=True).then_inc(acc_ready, 1)
                        G.up()
                    flush(nslots)

            def mla(l):
                t = 2 * l
                tok_major([(lambda k: (k // 4, k % 4), n, 2) for _, n in DCH], KT, h_hi, h_lo, 16 * t)
                pe.wait_ge(mla_in, 64)
                for q in range(4):
                    transposes([((hh * 2 + c) * P, ukr[:, c, (2 * q + hh) * P:(2 * q + hh + 1) * P])
                                for hh in range(2) for c in range(2)])
                pe.wait_ge(kv_ready, 1)
                for k in range(6):
                    def src(tt):
                        if k < 3:
                            return dtok[:, tt, k * P:(k + 1) * P]
                        return ckv[:, tt, (k - 3) * P:(k - 2) * P] if k < 5 else kr2[:, tt, :, :].rearrange("p a n -> p (a n)")
                    transposes([(tt * P, src(tt)) for tt in range(4)])
                    transposes([(0, src(4))])
                pe.wait_ge(lat_ready, 1)
                tok_major([(lambda k: (0, k), 256, 1)] * 2, 3, ql_hi, ql_lo, None)
                def absorb(h):
                    pe.wait_ge(acc_free, BANKS + nope_done[h])
                    for c in range(2):
                        for hf_ in range(2):
                            b = acc_bank()
                            mm(pb[:, b, 0:HALF], ukT[:, h, c * P:(c + 1) * P], qn[:, h % 2, half_cols(hf_)],
                               True, True).then_inc(acc_ready, 1)
                            G.up()
                nope_done = {}
                for h in range(HEADS):
                    (s,) = take_units(1)
                    for hf_ in range(2):
                        half_product(s, 3, hf_, (ql_hi, ql_lo))
                    flush(1)
                    nope_done[h] = G.v
                    if h:
                        absorb(h - 1)
                absorb(HEADS - 1)
                pe.wait_ge(qr_ready, 1)
                for q in range(4):
                    transposes([(tt * P, qrt[:, tt, q * P:(q + 1) * P]) for tt in range(4)])
                    transposes([(0, qrt[:, 4, q * P:(q + 1) * P])])
                for q in range(2):
                    transposes([(i * P, qrt[:, 4, (4 * q + i) * ROPE:(4 * q + i + 1) * ROPE]) for i in range(4)])
                pe.wait_ge(acc_free, G.v + BANKS)
                pe.wait_ge(aux_free, X.v + BANKS)
                def scores(n):
                    qb, h = divmod(n, HEADS)
                    N, q = (qb + 1) * P, slice(qb * P, (qb + 1) * P)
                    if n >= 2:
                        pe.wait_ge(sc_free, n - 1)
                    o = pb[:, 4 + n % 2, 0:N]
                    r = slice(h % 2 * ROPE, (h % 2 + 1) * ROPE)
                    for c in range(2):
                        mm(o, qaT[:, c, h, q], ckvT[:, c, 0:N], c == 0, False)
                    mm(o, qrT[r, h // 2, q], krT[r, 0:N], False, True).then_inc(sc_ready, 1)

                def contexts(n):
                    qb, h = divmod(n, HEADS)
                    pe.wait_ge(pt_copied, n + 1)
                    b = acc_bank()
                    for c in range(2):
                        for kb in range(qb + 1):
                            last = mm(pb[:, b, c * P:(c + 1) * P], ckv[:, kb, c * P:(c + 1) * P], pT[:, n % 2, kb, :],
                                      kb == 0, kb == qb)
                    last.then_inc(acc_ready, 1)
                    G.up()

                NA = 4 * HEADS
                scores(0)
                scores(1)
                for n in range(NA):
                    pe.wait_ge(p_ready, n + 1)
                    if n >= 2:
                        pe.wait_ge(pt_copied, n - 1)
                    for kb in range(n // HEADS + 1):
                        last = nc.tensor.transpose(pb[:, 6 + n % 2, kb * P:(kb + 1) * P],
                                                   pexp[:, n % 2, kb * P:(kb + 1) * P], ident[:])
                    last.then_inc(pt_ready, 1)
                    if n + 2 < NA:
                        scores(n + 2)
                    contexts(n)
                pe.wait_ge(sc_free, NA)
                pe.wait_ge(pt_copied, NA)
                for b_ in range(DEC_B):
                    pe.wait_ge(pg_full, 16 * 16 * (b_ + 1))
                    for c in range(2):
                        for q in range(2):
                            transposes([(i * P, pg[:, 4 * q + i, c * P:(c + 1) * P]) for i in range(4)])
                    for q in range(2):
                        transposes([(i * P, pgr[:, 4 * q + i, :]) for i in range(4)])
                    pe.wait_ge(aux_free, X.v + BANKS)
                    for q in range(3):
                        k0, k1 = (q * 512, (q + 1) * 512) if q < 2 else (TOK - P, TOK)
                        kc, kr_ = (pgT, pgrT) if q < 2 else (ckvT, krT)
                        b = aux_bank()
                        o = pb[0:R, b, 0:k1 - k0]
                        for c in range(2):
                            mm(o, qas[:, c, b_].rearrange("p h t -> p (h t)"), kc[:, c, k0:k1], c == 0, False)
                        mm(o, qrs[:, b_].rearrange("p h t -> p (h t)"), kr_[0:ROPE, k0:k1], False, True
                           ).then_inc(aux_ready, 1)
                        X.up()
                    pe.wait_ge(aux_free, X.v + BANKS)
                    transposes([(g * R, sp_[:, g * P:(g + 1) * P]) for g in range(8)])
                    transposes([(0, sp_[:, PAST:])])
                    pe.wait_ge(aux_free, X.v + BANKS)
                    b = aux_bank()
                    for g in range(PAGES + 1):
                        last = mm(pb[0:R, b, 0:KVR], spT[:, g, :], pg[:, g, :] if g < PAGES else ckv[:, 4, :],
                                  g == 0, g == PAGES)
                    last.then_inc(aux_ready, 1)
                    X.up()
                    pe.wait_ge(aux_free, X.v + BANKS)
                    transposes([(c * R, scx[:, c * P:(c + 1) * P]) for c in range(2)])
                pe.wait_ge(aux_free, X.v + BANKS)
                pe.wait_ge(acc_free, G.v + BANKS)
                pe.wait_ge(uv_full, 16)
                for h in range(HEADS):
                    for hf_ in range(2):
                        b = acc_bank()
                        for c in range(2):
                            last = mm(pb[:, b, 0:HALF], uv[:, c, h * P:(h + 1) * P], qaT[:, c, h, half_cols(hf_)],
                                      c == 0, c == 1)
                        last.then_inc(acc_ready, 1)
                        G.up()
                AR.up(16)
                down(KT)
                stats()

            for l in range(DEPTH):
                (gmlp, conv, mla)[l % 3](l)
                for n, (first, count) in enumerate(GU):
                    gate_up(count, 16 * (2 * l + 1))
                    AR.up(2 * count)
                    down(count)
                stats()
            pe.wait_ge(xa_ready, 16 * (2 * DEPTH + 1))
            for tt in range(TT):
                cols = slice(tt * P, min((tt + 1) * P, TOK))
                for q in range(2):
                    b = aux_bank()
                    for i in range(4):
                        last = nc.tensor.transpose(pb[0:cols.stop - cols.start, b, i * P:(i + 1) * P],
                                                   xa[:, 4 * q + i, cols], ident[:])
                    last.then_inc(aux_ready, 1)
                    X.up()

        @block.scalar
        def _(act):
            fn = nc.scalar.activation
            G, Q, SV, VNA, KA = Tally(), Tally(), Tally(), Tally(), Tally()

            act.wait_ge(coef_ready, 1)
            fn(cact[:].rearrange("p n k -> p (n k)"), par[:, C_C:C_END], ACT.Silu).then_inc(act_c, 1)
            act.wait_ge(coef_ready, 2)

            def apply(t):
                for h in range(2):
                    if t:
                        act.wait_ge(var_ready, SV.up())
                        fn(rstd[:, half_cols(h)], rstd[:, half_cols(h)], ACT.Sqrt, bias=epsl[:, 0:1]
                           ).then_inc(std_ready, 1)
                    n = 16 * t + 8 * h

                    def residual(m):
                        act.wait_ge(h_ready, n + m + 1)
                        fn(xa[:, m, half_cols(h)], xa[:, m, half_cols(h)], ACT.Identity,
                           scale=ag[:, t, m:m + 1], bias=ab[:, t, m:m + 1]).then_inc(xa_ready, 1)

                    w = HALF if h == 0 else HP
                    for m in range(KT):
                        act.wait_ge(n_ready, n + m + 1)
                        if n + m >= 2:
                            act.wait_ge(h_ready, n + m - 1)
                        fn(hf[:, m % 2, 0:w], xa[:, m, h * HALF:h * HALF + w], ACT.Identity,
                           scale=cs[:, t, m, 0:1], bias=cb[:, t, m, 0:1]).then_inc(hf_ready, 1)
                        if m:
                            residual(m - 1)
                    residual(KT - 1)

            def final():
                t = 2 * DEPTH
                for h in range(2):
                    act.wait_ge(var_ready, SV.up())
                    fn(rstd[:, half_cols(h)], rstd[:, half_cols(h)], ACT.Sqrt, bias=epsl[:, 0:1]
                       ).then_inc(std_ready, 1)
                    for m in range(KT):
                        act.wait_ge(n_ready, 16 * t + 8 * h + m + 1)
                        fn(xa[:, m, half_cols(h)], xa[:, m, half_cols(h)], ACT.Identity,
                           scale=ag[:, t, m:m + 1], bias=ab[:, t, m:m + 1]).then_inc(xa_ready, 1)

            def down(last):
                with rolled(act, 2, (G, 8), (Q, 8)) as i:
                    for mm_ in range(4):
                        for h in range(2):
                            if last:
                                act.wait_ge(acc_free, G.v + 1 + BANKS)
                                act.wait_ge(q_done, Q.v + 1)
                                settle(act, act_passed)
                                fn(sqt[:, h, :], one(xa, i * 4 + mm_, half_cols(h)), ACT.Square
                                   ).then_inc(sq_ready, 1)
                            G.up()
                            Q.up()
                if not last:
                    Q.up(-16)

            def gates(trips, func, bias=None, after=None, steps=()):
                with rolled(act, trips, (G, 8), *steps) as i:
                    for m in range(2):
                        for h in range(2):
                            act.wait_ge(acc_free, G.v - 2 + BANKS)
                            g = G.v + (1 if bias is None else 2)
                            act.wait_ge(acc_ready, g)
                            if bias is not None:
                                settle(act, act_passed)
                            b = (G.n + (0 if bias is None else 1)) % BANKS
                            kw = {} if bias is None else {"bias": bias(i * 2 + m)}
                            fn(sg[:, h, :], pb[:, b, 0:HALF], func, **kw).then_inc(sg_ready, 1)
                            G.up(2)
                    if after:
                        after(i)

            def gmlp(l):
                with rolled(act, 2, (G, 20)) as i:
                    for gg in range(4):
                        for tt in range(TT):
                            act.wait_ge(acc_ready, G.v + 1)
                            settle(act, act_passed)
                            fn(v_sb[:, tt, bass.ds(i * 1024 + gg * 256, 256)], pb[:, G.n % BANKS, 0:256], ACT.Gelu
                               ).then_inc(v_ready, 1)
                            G.up()
                act.wait_ge(var_ready, SV.up())
                fn(vrs[:], bag[:, :, 1], ACT.Sqrt, bias=epsl[:, 0:1]).then_inc(std_ready, 1)
                for ph in range(2):
                    with rolled(act, 2, (G, 8), (KA, 8), (VNA, 2)) as i:
                        for gg in range(2):
                            act.wait_ge(vn_ready, VNA.up())
                            act.dma_start(O["new_gmlp_v_sample"][l // 3].rearrange("b t c -> (b t) c")
                                          [:, bass.ds((i * 2 + (4 * ph + gg)) * 256, 256)],
                                          vn[NS:P, gg, 4, :]).then_inc(vo_done[gg], 16)
                            for mt in range(2):
                                for h in range(2):
                                    act.wait_ge(acc_ready, G.v + 1)
                                    act.wait_ge(a_ready, KA.v + 7)
                                    fn(u_sb[:, half_cols(h)], pb[:, G.n % BANKS, 0:HALF], ACT.Gelu
                                       ).then_inc(sg_ready, 1)
                                    G.up()
                                    KA.up()
                    down(ph == 1)

            def conv(l):
                YC = Tally()

                def squares(i):
                    for m in range(2):
                        act.wait_ge(yc_ready, YC.up())
                        for h in range(2):
                            act.wait_ge(q_done, Q.v + 1)
                            settle(act, act_passed)
                            fn(sqt[:, h, :], one(yc, i * 2 + m, half_cols(h)), ACT.Square).then_inc(sq_ready, 1)
                            Q.up()

                gates(4, ACT.Sigmoid, lambda j: one1(par, j, C_PW1 + KT), squares, ((Q, 4), (YC, 2)))
                act.wait_ge(st_ready, 1)
                act.dma_start(O["new_conv_prompt"][0, 0], st_p[:]).then_inc(out_done, 16)
                act.dma_start(O["new_conv_sample"][0, :, CTX - DEC_T:, :], st_s[:]).then_inc(out_done, 16)
                for h in range(2):
                    act.wait_ge(var_ready, SV.up())
                    fn(rstd[:, half_cols(h)], rstd[:, half_cols(h)], ACT.Sqrt, bias=epsl[:, 0:1]
                       ).then_inc(std_ready, 1)
                    for m in range(KT):
                        act.wait_ge(yc_ready, KT + 8 * h + m + 1)
                        act.wait_ge(a_ready, KA.v + 8 - 1)
                        fn(hf[:, m % 2, :], yc[:, m, half_cols(h)], ACT.Silu, scale=par[:, C_CG + m:C_CG + m + 1],
                           bias=par[:, C_CB + m:C_CB + m + 1]).then_inc(hf_ready, 1)
                        KA.up()
                down(True)

            def mla(l):
                G.up(15)
                act.wait_ge(d_ready, 1)
                act.wait_ge(out_done, OUTS * 16)
                for tt in range(TT):
                    fn(qaT[:, 1, tt, 0:QR], dtok[:, tt, 0:QR], ACT.Square, accum_out=ssq[:, tt, 0:1])
                    fn(qaT[:, 0, tt, 0:KVR], dtok[:, tt, QR:QR + KVR], ACT.Square, accum_out=ssq[:, tt, 1:2])
                act.drain()
                for n, width in enumerate((QR, KVR)):
                    last = fn(ssq[:, :, n], ssq[:, :, n], ACT.Sqrt, scale=1.0 / width, bias=epsl[:, 1:2])
                last.then_inc(ssq_ready, 1)
                act.wait_ge(kv_ready, 1)
                o_ckv, o_kr = O["new_ckv_prompt"][0, 0], O["new_krope_prompt"][0, 0]
                act.dma_start(o_ckv.rearrange("(t p) c -> p t c", p=P), ckv[:, 0:4, :]).then_inc(kv_out, 16)
                act.dma_start(o_kr.rearrange("(t p) c -> p t c", p=P), kr2[:, 0:4, 0, :]).then_inc(kv_out, 16)
                act.dma_start(O["new_ckv_sample"][0].rearrange("b t c -> (b t) c"), ckv[NS:P, 4, :]
                              ).then_inc(kv_out, 16)
                act.dma_start(O["new_krope_sample"][0].rearrange("b t c -> (b t) c"), kr2[NS:P, 4, 0, :]
                              ).then_inc(kv_out, 16)
                G.up(10 + 6 * HEADS)
                NA = 4 * HEADS

                def expo(n):
                    N = (n // HEADS + 1) * P
                    act.wait_ge(nm_ready, n + 1)
                    if n >= 2:
                        act.wait_ge(pt_ready, n - 1)
                    fn(pexp[:, n % 2, 0:N], pb[:, 4 + n % 2, 0:N], ACT.Exp, scale=SCALE, bias=att[:, n % 2, 0:1],
                       accum_out=att[:, n % 2, 1:2])
                    act.drain().then_inc(sc_free, 1)

                expo(0)
                for n in range(NA):
                    if n + 1 < NA:
                        expo(n + 1)
                    N = (n // HEADS + 1) * P
                    act.wait_ge(pt_ready, n + 1)
                    if n >= 2:
                        act.wait_ge(acc_ready, G.v - 1)
                    fn(pT[:, n % 2, :, :].rearrange("p k q -> p (k q)")[:, 0:N], pb[:, 6 + n % 2, 0:N], ACT.Copy
                       ).then_inc(pt_copied, 1)
                    G.up()
                for b in range(DEC_B):
                    act.wait_ge(nm_ready, NA + b + 1)
                    for q in range(3):
                        k0, k1 = (q * 512, (q + 1) * 512) if q < 2 else (PAST, PAST + P)
                        fn(sp_[:, k0:k1], pb[0:R, SAMPLE_BANK(b, q), 0:k1 - k0], ACT.Exp, scale=SCALE,
                           bias=satt[:, 0:1], accum_out=satt[:, 1 + q:2 + q])
                    act.drain().then_inc(se_ready, 1)
                G.up(2 * HEADS)
                KA.up(16)
                down(True)

            apply(0)
            for l in range(DEPTH):
                (gmlp, conv, mla)[l % 3](l)
                apply(2 * l + 1)
                for n, (first, count) in enumerate(GU):
                    gates(count // 2, ACT.Silu)
                    KA.up(2 * count)
                    down(n == 2)
                if l < DEPTH - 1:
                    apply(2 * l + 2)
                else:
                    final()

        @block.vector
        def _(dve):
            v = nc.vector
            G, X, SG = Tally(), Tally(), Tally()
            ST, SQ, GB = Tally(), Tally(), [Tally(), Tally()]

            def aux():
                dve.wait_ge(aux_ready, X.v + 1)
                b = BANKS + X.n % BANKS
                X.up()
                return b

            def split(hi, lo, src):
                v.tensor_copy(hi, src)
                dve.drain()
                return v.tensor_tensor(lo, src, hi.bitcast(F32), ALU.subtract)

            dve.sem_inc(acc_free, BANKS)
            dve.sem_inc(aux_free, BANKS)
            dve.sem_inc(a_ready, 8)
            dve.sem_inc(q_done, 2)
            for n in range(2):
                dve.sem_inc(vo_done[n], 16)
            v.memset(ones[:], 1.0 / D)
            v.memset(epsl[:, 0:1], LN_EPS)
            v.memset(epsl[:, 1:2], RMS_EPS)
            dve.drain().then_inc(const_made, 1)
            for c0, rows in ((C_ADA, P), (C_ADA + P, DEPTH * ADA_M - P), (C_LN, P), (C_PW1, C_END - C_PW1)):
                v.tensor_copy(par[:, c0:c0 + rows], pb[:, aux(), 0:rows]).then_inc(aux_free, 1)
            dve.drain().then_inc(coef_ready, 1)
            for tt in range(TT):
                n = P if tt < 4 else NS
                for q in range(2):
                    v.tensor_copy(xa[:, 4 * q:4 * q + 4, tt * P:tt * P + n],
                                  pb[:, aux(), :].rearrange("p (m t) -> p m t", m=4)[:, :, 0:n]
                                  ).then_inc(aux_free, 1)
            v.memset(ag[:, 0, :], ALPHA)
            v.memset(ab[:, 0, :], 0.0)

            def ln_rows(kind, l):
                c0 = C_LN + 32 * kind + KT * l
                return par[:, c0:c0 + KT]

            for l in range(DEPTH):
                with rolled(dve, 6, (X, 4)) as i:
                    for c in range(2):
                        v.tensor_copy(ada_row[:, c, :], pb[0:NC, aux(), :]).then_inc(aux_free, 1)
                        b = aux()
                        v.tensor_tensor(mod[:, bass.ds(i * 8 + c * 4, 4), :],
                                        pb[:, b, 0:4 * NC].rearrange("p (m n) -> p m n", m=4),
                                        par[:, bass.ds(i * 8 + (c * 4 + ADA_M * l), 4)].unsqueeze(2)
                                        .to_broadcast([P, 4, NC]), ALU.add).then_inc(aux_free, 1)
                dve.drain()
                part = [mod[:, KT * n:KT * (n + 1), :] for n in range(6)]
                for n in range(2):
                    t = 2 * l + n
                    shift, scale, g = part[3 * n:3 * n + 3]
                    v.tensor_copy(gate[:, t], g)
                    if t:
                        gain, bias = [ln_rows(2 * (1 - n) + e, l - 1 + n).unsqueeze(2).to_broadcast([P, KT, NC])
                                      for e in range(2)]
                        v.scalar_tensor_tensor(out=cs[:, t], in0=scale, scalar=1.0, in1=gain, op0=ALU.add, op1=ALU.mult)
                        v.scalar_tensor_tensor(out=cb[:, t], in0=scale, scalar=1.0, in1=bias, op0=ALU.add, op1=ALU.mult)
                        dve.drain()
                        v.tensor_tensor(cb[:, t], cb[:, t], shift, ALU.add)
                        v.tensor_scalar(ag[:, t, :], ln_rows(2 * (1 - n), l - 1 + n), ALPHA, None, ALU.mult)
                        v.tensor_scalar(ab[:, t, :], ln_rows(2 * (1 - n) + 1, l - 1 + n), ALPHA, None, ALU.mult)
                    else:
                        v.tensor_scalar(cs[:, t], scale, 1.0, None, ALU.add)
                        v.tensor_copy(cb[:, t], shift)
                dve.drain()
            v.tensor_copy(ag[:, 2 * DEPTH, :], ln_rows(2, DEPTH - 1))
            v.tensor_copy(ab[:, 2 * DEPTH, :], ln_rows(3, DEPTH - 1))
            dve.drain().then_inc(coef_ready, 1)
            dve.drain().then_inc(n_ready, 16)

            def statistics(h):
                cols = half_cols(h)
                v.tensor_copy(mean[:, cols], pb[:, aux(), 0:HALF]).then_inc(aux_free, 1)
                dve.drain()
                v.tensor_tensor(sqt[:, h, :], mean[:, cols], mean[:, cols], ALU.mult)
                dve.drain()
                v.tensor_tensor(rstd[:, cols], pb[:, aux(), 0:HALF], sqt[:, h, :], ALU.subtract).then_inc(aux_free, 1)
                dve.drain()
                v.tensor_scalar(rstd[:, cols], rstd[:, cols], 0.0, None, ALU.max).then_inc(var_ready, 1)
                dve.wait_ge(std_ready, ST.up())
                v.reciprocal(rstd[:, cols], rstd[:, cols])
                dve.drain()

            def normalise(x, cols, sem_):
                v.tensor_tensor(x, x, mean[:, cols], ALU.subtract)
                dve.drain()
                v.tensor_tensor(x, x, rstd[:, cols], ALU.mult).then_inc(sem_, 1)

            def apply(t):
                for h in range(2):
                    if t:
                        statistics(h)
                        normalise(xa[:, 0, half_cols(h)], half_cols(h), n_ready)
                    for m in range(KT):
                        if t and m + 1 < KT:
                            normalise(xa[:, m + 1, half_cols(h)], half_cols(h), n_ready)
                        if h:
                            _, sc = per_row(cs, t, m)
                            _, sh = per_row(cb, t, m)
                            o = bt(hf[:, m % 2, HP:HALF])
                            dve.drain()
                            v.tensor_tensor(o, bt(xa[:, m, SEQ:TOK]), sc, ALU.mult)
                            dve.drain()
                            v.tensor_tensor(o, o, sh, ALU.add)
                            dve.drain()
                        dve.wait_ge(hf_ready, HF.up())
                        split(h_hi[:, m, half_cols(h)], h_lo[:, m, half_cols(h)], hf[:, m % 2, :]).then_inc(h_ready, 1)

            HF = Tally()

            def final():
                for h in range(2):
                    statistics(h)
                    for m in range(KT):
                        normalise(xa[:, m, half_cols(h)], half_cols(h), n_ready)

            def clear_sums():
                v.memset(s_sum[:], 0.0)
                v.memset(s_sq[:], 0.0)
                dve.drain()

            def add_sums(y, h):
                v.tensor_tensor(s_sum[:, half_cols(h)], s_sum[:, half_cols(h)], y, ALU.add)
                dve.wait_ge(sq_ready, SQ.up())
                v.tensor_tensor(s_sq[:, half_cols(h)], s_sq[:, half_cols(h)], sqt[:, h, :], ALU.add
                                ).then_inc(q_done, 1)

            def down(e, last):
                dve.wait_ge(xa_ready, 16 * (e + 1))
                if last:
                    clear_sums()
                with rolled(dve, 2, (G, 8), *(((SQ, 8),) if last else ())) as i:
                    for mm_ in range(4):
                        m = i * 4 + mm_
                        gp, gs = per_row(gate, e, m)
                        for h in range(2):
                            if h:
                                dve.drain()
                            dve.wait_ge(acc_ready, G.v + 1)
                            ps = pb[:, G.n % BANKS, 0:HALF]
                            w = HALF if h == 0 else HP
                            y = one(xa, m, slice(h * HALF, h * HALF + w))
                            if h:
                                v.tensor_tensor(bt(smt[:]), bt(ps[:, HP:HALF]), gs, ALU.mult)
                            last_ = v.scalar_tensor_tensor(out=y, in0=ps[:, 0:w], scalar=gp, in1=y,
                                                           op0=ALU.mult, op1=ALU.add)
                            if h:
                                dve.drain()
                                ys = one(xa, m, slice(SEQ, TOK))
                                last_ = v.tensor_tensor(ys, ys, smt[:], ALU.add)
                            last_.then_inc(acc_free, 1)
                            if last:
                                dve.drain()
                                add_sums(one(xa, m, half_cols(h)), h)
                            G.up()

            def gate_up(count):
                with rolled(dve, count // 2, (G, 8), (SG, 4)) as i:
                    for mm_ in range(2):
                        m = i * 2 + mm_
                        for h in range(2):
                            dve.wait_ge(acc_ready, G.v + 2)
                            dve.wait_ge(sg_ready, SG.up())
                            v.tensor_tensor(pr[:, h, :], pb[:, (G.n + 1) % BANKS, 0:HALF], sg[:, h, :], ALU.mult
                                            ).then_inc(acc_free, 2)
                            dve.drain()
                            split(one(a_hi, m, half_cols(h)), one(a_lo, m, half_cols(h)), pr[:, h, :]
                                  ).then_inc(a_ready, 1)
                            G.up(2)

            def gmlp(l):
                j = l // 3
                v.memset(wss_raw[:], 0.0).then_inc(ws_zero, 1)
                with rolled(dve, 2, (G, 20), (VV, 20)) as i:
                    for gg in range(4):
                        for tt in range(TT):
                            dve.wait_ge(v_ready, VV.up())
                            v.bn_stats(one(bst[:, tt], i * 4 + gg),
                                       v_sb[:, tt, bass.ds(i * 1024 + gg * 256, 256)]).then_inc(acc_free, 1)
                            G.up()
                dve.drain()
                for tt in range(TT):
                    v.bn_aggr(bag[:, tt, :], bst[:, tt].rearrange("p g s -> p (g s)"))
                dve.drain().then_inc(var_ready, 1)
                dve.wait_ge(ws_in, 160 * (j + 1))
                v.tensor_tensor(ws_raw[:], ws_raw[:], tril[:].unsqueeze(1).to_broadcast([P, GROUPS, P]), ALU.mult)
                v.tensor_tensor(wss_raw[:, :, NS:], wss_raw[:, :, NS:],
                                tril[0:NS, 0:NS].unsqueeze(1).to_broadcast([NS, GROUPS, NS]), ALU.mult)
                dve.drain().then_inc(ws_ready, 1)
                dve.wait_ge(std_ready, ST.up())
                v.reciprocal(vrs[:], vrs[:])
                dve.drain()
                for q in range(2):
                    v.tensor_copy(wsT[:, 4 * q:4 * q + 4, :].rearrange("p g t -> p (g t)"), pb[:, aux(), :]
                                  ).then_inc(aux_free, 1)
                v.tensor_copy(wssT[:].rearrange("p g t -> p (g t)"), pb[:, aux(), :]).then_inc(aux_free, 1)
                for ph in range(2):
                    with rolled(dve, 2, (G, 8), (X, 8), (SG, 8), (GB[0], 48), (GB[1], 48), (VO, 16)) as i:
                        for gg in range(2):
                            g = i * 2 + (4 * ph + gg)
                            dve.wait_ge(gb_full[gg], GB[gg].up(48))
                            dve.wait_ge(vo_done[gg], VO.v + 16)
                            for tt in range(TT):
                                v.tensor_scalar(vn[:, gg, tt, :], v_sb[:, tt, bass.ds(g * 256, 256)],
                                                bag[:, tt, 0:1], vrs[:, tt:tt + 1], ALU.subtract, ALU.mult)
                            for n, op in enumerate((ALU.mult, ALU.add)):
                                dve.drain()
                                last_ = v.tensor_tensor(vn[:, gg], vn[:, gg],
                                                        gbt[:, gg, n, :].unsqueeze(1).to_broadcast([P, TT, 256]), op)
                            last_.then_inc(vn_ready, 1)
                            for mt in range(2):
                                m = i * 4 + (2 * gg + mt)
                                bp, bs_ = aux(), aux()
                                dve.wait_ge(aux_ready, X.v)
                                pp = pb[:, bp, :].rearrange("p (c t) -> p c t", c=4)
                                v.tensor_tensor(pp, pp, bsb[:, gg, :].unsqueeze(1).to_broadcast([P, 4, P]), ALU.add)
                                ps = bt(pb[:, bs_, 0:NS])
                                v.tensor_tensor(ps, ps, bsb[:, gg, 0:DEC_T].unsqueeze(1)
                                                .to_broadcast([P, DEC_B, DEC_T]), ALU.add)
                                dve.drain()
                                for h in range(2):
                                    dve.wait_ge(sg_ready, SG.up())
                                    if h == 0:
                                        v.tensor_tensor(u_sb[:, 0:HALF], u_sb[:, 0:HALF], pb[:, bp, 0:HALF], ALU.mult)
                                    else:
                                        v.tensor_tensor(u_sb[:, HALF:SEQ], u_sb[:, HALF:SEQ], pb[:, bp, HALF:SEQ],
                                                        ALU.mult).then_inc(aux_free, 1)
                                        v.tensor_tensor(u_sb[:, SEQ:], u_sb[:, SEQ:], pb[:, bs_, 0:NS], ALU.mult
                                                        ).then_inc(aux_free, 1)
                                    dve.drain().then_inc(acc_free, 1)
                                    split(one(a_hi, m, half_cols(h)), one(a_lo, m, half_cols(h)), u_sb[:, half_cols(h)]
                                          ).then_inc(a_ready, 1)
                                    G.up()
                            if gg:
                                VO.up(16)
                    if ph:
                        for n in range(2):
                            dve.wait_ge(vo_done[n], VO.v + 16)
                    down(2 * l, ph == 1)

            VV, VO = Tally(), Tally()

            def conv(l):
                v.memset(full[:, :, 0:CTX], 0.0)
                v.tensor_copy(wdT[:].rearrange("p k w -> p (k w)"), pb[:, aux(), 0:KT * CW]).then_inc(aux_free, 1)
                for m in range(KT):
                    v.tensor_copy(stT[:, m, :], pb[:, aux(), 0:DEC_B * CTX]).then_inc(aux_free, 1)
                clear_sums()
                with rolled(dve, 4, (G, 8), (X, 4), (SG, 4), (SQ, 4)) as i:
                    for mm_ in range(2):
                        m = i * 2 + mm_
                        fs = full_s(full[:, mm_, :])
                        v.tensor_copy(fs[:, :, 0:CTX], one(stT, m).rearrange("p (b r) -> p b r", b=DEC_B))
                        b1 = one1(par, m, C_PW1)
                        for h in range(2):
                            dve.wait_ge(acc_ready, G.v + 2)
                            dve.wait_ge(sg_ready, SG.up())
                            ps = pb[:, G.n % BANKS, 0:HALF]
                            w = HALF if h == 0 else HP
                            if h:
                                v.scalar_tensor_tensor(out=snew[:, mm_, :], in0=ps[:, HP:HALF], scalar=b1,
                                                       in1=sg[:, 1, HP:HALF], op0=ALU.add, op1=ALU.mult)
                            v.scalar_tensor_tensor(out=full[:, mm_, CTX + h * HALF:CTX + h * HALF + w],
                                                   in0=ps[:, 0:w], scalar=b1, in1=sg[:, h, 0:w],
                                                   op0=ALU.add, op1=ALU.mult).then_inc(acc_free, 2)
                            G.up(2)
                        dve.drain()
                        v.tensor_copy(fs[:, :, CTX:], bt(snew[:, mm_, :]))
                        dve.drain().then_inc(full_ready, 1)
                        yp, ys = one(yc, m, slice(0, SEQ)), bt(one(yc, m, slice(SEQ, TOK)))
                        for k in range(CW):
                            w1 = one(wdT, m, slice(k, k + 1))
                            xp, xs = full[:, mm_, k:k + SEQ], fs[:, :, k:k + DEC_T]
                            if k == 0:
                                bd = one1(par, m, C_DW)
                                v.tensor_scalar(yp, xp, w1, bd, ALU.mult, ALU.add)
                                v.tensor_scalar(ys, xs, w1, bd, ALU.mult, ALU.add)
                            else:
                                v.scalar_tensor_tensor(out=yp, in0=xp, scalar=w1, in1=yp, op0=ALU.mult, op1=ALU.add)
                                v.scalar_tensor_tensor(out=ys, in0=xs, scalar=w1, in1=ys, op0=ALU.mult, op1=ALU.add)
                            dve.drain()
                        dve.drain().then_inc(yc_ready, 1)
                        for h in range(2):
                            add_sums(one(yc, m, half_cols(h)), h)
                    for mm_ in range(2):
                        m = i * 2 + mm_
                        for dst, n in ((st_p, CTX), (st_s, NS)):
                            v.tensor_copy(dst[:, bass.ds(m * P, P)], pb[0:n, aux(), 0:P]).then_inc(aux_free, 1)
                dve.drain().then_inc(st_ready, 1)
                dve.wait_ge(xa_ready, 16 * (2 * l + 1))
                v.tensor_tensor(gbw[:], gate[:, 2 * l], par[:, C_PW2:C_PW2 + KT].unsqueeze(2)
                                .to_broadcast([P, KT, NC]), ALU.mult)
                dve.drain()
                for m in range(KT):
                    v.tensor_scalar(xa[:, m, 0:SEQ], xa[:, m, 0:SEQ], gbw[:, m, 0:1], None, ALU.add)
                    v.tensor_tensor(bt(xa[:, m, SEQ:]), bt(xa[:, m, SEQ:]),
                                    gbw[:, m, 1:NC].unsqueeze(2).to_broadcast([P, DEC_B, DEC_T]), ALU.add)
                for h in range(2):
                    statistics(h)
                    cols = half_cols(h)
                    normalise(yc[:, 0, cols], cols, yc_ready)
                    for m in range(KT):
                        if m + 1 < KT:
                            normalise(yc[:, m + 1, cols], cols, yc_ready)
                        dve.wait_ge(hf_ready, HF.up())
                        split(a_hi[:, m, cols], a_lo[:, m, cols], hf[:, m % 2, :]).then_inc(a_ready, 1)
                down(2 * l, True)

            def mla(l):
                half = ROPE // 2
                for c0, n in DCH:
                    for tt in range(TT):
                        dve.wait_ge(acc_ready, G.v + 1)
                        v.tensor_copy(dtok[:, tt, c0:c0 + n], pb[:, G.n % BANKS, 0:n]).then_inc(acc_free, 1)
                        G.up()
                dve.drain().then_inc(d_ready, 1)
                for q in range(4):
                    v.tensor_copy(ukT[:, 2 * q:2 * q + 2, :].rearrange("p h c -> p (h c)"), pb[:, aux(), :]
                                  ).then_inc(aux_free, 1)
                dve.wait_ge(mla_in, 64)
                dve.wait_ge(ssq_ready, 1)
                v.reciprocal(ssq[:], ssq[:])
                dve.drain()
                for tt in range(TT):
                    v.scalar_tensor_tensor(out=dtok[:, tt, 0:QR], in0=dtok[:, tt, 0:QR], scalar=ssq[:, tt, 0:1],
                                           in1=gqk[:, 0:QR], op0=ALU.mult, op1=ALU.mult)
                    v.scalar_tensor_tensor(out=ckv[:, tt, :], in0=dtok[:, tt, QR:QR + KVR], scalar=ssq[:, tt, 1:2],
                                           in1=gqk[:, QR:], op0=ALU.mult, op1=ALU.mult)
                cos, sin = rtab[:, :, 0:half], rtab[:, :, half:]
                x1, x2 = dtok[:, :, QR + KVR:QR + KVR + half], dtok[:, :, QR + KVR + half:]
                ra, rb = [rt[:, n, 0:TT * half].rearrange("p (t r) -> p t r", t=TT) for n in range(2)]
                v.tensor_tensor(ra, x1, cos, ALU.mult)
                v.tensor_tensor(rb, x2, sin, ALU.mult)
                dve.drain()
                v.tensor_tensor(kr2[:, :, 0, 0:half], ra, rb, ALU.subtract)
                dve.drain()
                v.tensor_tensor(ra, x2, cos, ALU.mult)
                v.tensor_tensor(rb, x1, sin, ALU.mult)
                dve.drain()
                v.tensor_tensor(kr2[:, :, 0, half:], ra, rb, ALU.add)
                dve.drain()
                v.tensor_copy(kr2[:, :, 1, :], kr2[:, :, 0, :])
                dve.drain().then_inc(kv_ready, 1)
                for k in range(6):
                    for n, (cols, src) in enumerate(((slice(0, SEQ), slice(0, SEQ)), (slice(SEQ, TOK), slice(NS, P)))):
                        ps = pb[:, aux(), src]
                        if k < 3:
                            split(ql_hi[:, k, cols], ql_lo[:, k, cols], ps).then_inc(aux_free, 1)
                        else:
                            v.tensor_copy(ckvT[:, k - 3, cols] if k < 5 else krT[:, cols], ps).then_inc(aux_free, 1)
                dve.drain().then_inc(lat_ready, 1)
                for c in range(2):
                    for tt in range(TT):
                        dve.wait_ge(acc_ready, G.v + 1)
                        v.tensor_copy(qrt[:, tt, c * 256:(c + 1) * 256], pb[:, G.n % BANKS, 0:256]
                                      ).then_inc(acc_free, 1)
                        G.up()

                def rotate(tt):
                    q4 = qrt[:, tt, :].rearrange("p (h r) -> p h r", h=HEADS)
                    x1, x2 = q4[:, :, 0:half], q4[:, :, half:]
                    ra, rb = [rt[:, n, :].rearrange("p (h r) -> p h r", h=HEADS) for n in range(2)]
                    cos, sin = [rtab[:, tt, n * half:(n + 1) * half].unsqueeze(1).to_broadcast([P, HEADS, half])
                                for n in range(2)]
                    dve.drain()
                    v.tensor_tensor(ra, x1, cos, ALU.mult)
                    v.tensor_tensor(rb, x2, sin, ALU.mult)
                    dve.drain()
                    v.tensor_tensor(ra, ra, rb, ALU.subtract)
                    v.tensor_tensor(x2, x2, cos, ALU.mult)
                    dve.drain()
                    v.tensor_tensor(rb, x1, sin, ALU.mult)
                    dve.drain()
                    v.tensor_tensor(x2, x2, rb, ALU.add)
                    v.tensor_copy(x1, ra)

                def evac_q(h, hf_):
                    dve.wait_ge(acc_ready, G.v + 1)
                    v.tensor_copy(qn[:, h % 2, half_cols(hf_)], pb[:, G.n % BANKS, 0:HALF]).then_inc(acc_free, 1)
                    G.up()

                def evac_absorbed(h):
                    for c in range(2):
                        for hf_ in range(2):
                            dve.wait_ge(acc_ready, G.v + 1)
                            ps = pb[:, G.n % BANKS, 0:HALF]
                            w = HP if hf_ else HALF
                            if hf_:
                                v.tensor_copy(qas[:, c, :, h, :], bt(ps[:, HP:]))
                            v.tensor_copy(qaT[:, c, h, hf_ * HALF:hf_ * HALF + w], ps[:, 0:w]).then_inc(acc_free, 1)
                            G.up()

                for h in range(HEADS):
                    for hf_ in range(2):
                        evac_q(h, hf_)
                    if h:
                        evac_absorbed(h - 1)
                    if h < TT:
                        rotate(h)
                    elif h == TT:
                        dve.drain().then_inc(qr_ready, 1)
                evac_absorbed(HEADS - 1)
                for q in range(4):
                    v.tensor_copy(qrT[:, q, 0:SEQ], pb[:, aux(), :]).then_inc(aux_free, 1)
                    v.tensor_copy(qrT[:, q, SEQ:], pb[:, aux(), NS:P]).then_inc(aux_free, 1)
                for q in range(2):
                    ps = pb[0:ROPE, aux(), :].rearrange("p (h t) -> p h t", h=4)
                    for i in range(4):
                        last_ = v.tensor_copy(qrs[:, :, 4 * q + i, :], bt(ps[:, i, NS:]))
                    last_.then_inc(aux_free, 1)
                dve.wait_ge(mask_in, 32)
                NA = 4 * HEADS

                def maxima(n):
                    qb = n // HEADS
                    dve.wait_ge(sc_ready, n + 1)
                    ps = pb[:, 4 + n % 2, :]
                    diag = ps[:, qb * P:(qb + 1) * P]
                    v.tensor_tensor(diag, diag, cmask[:], ALU.add)
                    dve.drain()
                    v.reduce_max(att[:, n % 2, 3:4], ps[:, 0:(qb + 1) * P], AX.X)
                    dve.drain()
                    v.tensor_scalar(att[:, n % 2, 0:1], att[:, n % 2, 3:4], -SCALE, None, ALU.mult
                                    ).then_inc(nm_ready, 1)

                def scale_rows(n):
                    N = (n // HEADS + 1) * P
                    dve.wait_ge(sc_free, n + 1)
                    v.reciprocal(att[:, n % 2, 2:3], att[:, n % 2, 1:2])
                    dve.drain()
                    v.tensor_scalar(pexp[:, n % 2, 0:N], pexp[:, n % 2, 0:N], att[:, n % 2, 2:3], None, ALU.mult
                                    ).then_inc(p_ready, 1)

                def evac_context(n):
                    qb, h = divmod(n, HEADS)
                    dve.wait_ge(acc_ready, G.v + 1)
                    v.tensor_copy(qaT[:, :, h, qb * P:(qb + 1) * P],
                                  pb[:, G.n % BANKS, 0:2 * P].rearrange("p (c q) -> p c q", c=2)).then_inc(acc_free, 1)
                    G.up()

                maxima(0)
                for n in range(NA):
                    if n + 1 < NA:
                        maxima(n + 1)
                    scale_rows(n)
                    if n:
                        evac_context(n - 1)
                evac_context(NA - 1)
                for b in range(DEC_B):
                    for c in range(2):
                        for q in range(2):
                            v.tensor_copy(pgT[:, c, q * 512:(q + 1) * 512], pb[:, aux(), :]).then_inc(aux_free, 1)
                    for q in range(2):
                        v.tensor_copy(pgrT[:, q * 512:(q + 1) * 512], pb[0:ROPE, aux(), :]).then_inc(aux_free, 1)
                    banks = [aux() for _ in range(3)]
                    assert banks == [SAMPLE_BANK(b, q) for q in range(3)]
                    m_ = pb[0:R, banks[2], 0:P]
                    v.tensor_tensor(m_, m_, smask[:, b, :], ALU.add)
                    dve.drain()
                    for q in range(3):
                        v.reduce_max(satt[:, 5 + q:6 + q], pb[0:R, banks[q], 0:512 if q < 2 else P], AX.X)
                    dve.drain()
                    v.reduce_max(satt[:, 4:5], satt[:, 5:8], AX.X)
                    dve.drain()
                    v.tensor_scalar(satt[:, 0:1], satt[:, 4:5], -SCALE, None, ALU.mult).then_inc(nm_ready, 1)
                    dve.wait_ge(se_ready, b + 1)
                    v.reduce_sum(satt[:, 4:5], satt[:, 1:4], AX.X)
                    dve.drain()
                    v.reciprocal(satt[:, 4:5], satt[:, 4:5])
                    dve.drain()
                    v.tensor_scalar(sp_[:], sp_[:], satt[:, 4:5], None, ALU.mult).then_inc(aux_free, 3)
                    v.tensor_copy(spT[:, 0:8, :].rearrange("p g r -> p (g r)"), pb[:, aux(), :]).then_inc(aux_free, 1)
                    v.tensor_copy(spT[:, 8, :], pb[:, aux(), 0:R]).then_inc(aux_free, 1)
                    v.tensor_copy(scx[:], pb[0:R, aux(), 0:KVR]).then_inc(aux_free, 1)
                    dve.drain().then_inc(pg_used, 1)
                    bk = aux()
                    for c in range(2):
                        last_ = v.tensor_copy(qaT[:, c, :, SEQ + DEC_T * b:SEQ + DEC_T * (b + 1)],
                                              pb[:, bk, c * R:(c + 1) * R].rearrange("p (h t) -> p h t", h=HEADS))
                    last_.then_inc(aux_free, 1)
                for h in range(HEADS):
                    for hf_ in range(2):
                        dve.wait_ge(acc_ready, G.v + 1)
                        split(a_hi[:, h, half_cols(hf_)], a_lo[:, h, half_cols(hf_)], pb[:, G.n % BANKS, 0:HALF]
                              ).then_inc(acc_free, 1)
                        dve.drain().then_inc(a_ready, 1)
                        G.up()
                dve.wait_ge(kv_out, 64)
                down(2 * l, True)

            apply(0)
            for l in range(DEPTH):
                (gmlp, conv, mla)[l % 3](l)
                apply(2 * l + 1)
                for n, (first, count) in enumerate(GU):
                    gate_up(count)
                    down(2 * l + 1, n == 2)
                if l < DEPTH - 1:
                    apply(2 * l + 2)
                else:
                    final()
            for tt in range(TT):
                n = P if tt < 4 else NS
                if tt >= 2:
                    dve.wait_ge(y_out[tt % 2], 16 * (tt // 2))
                for q in range(2):
                    v.tensor_copy(yo[0:n, tt % 2, q * 512:(q + 1) * 512], pb[0:n, aux(), :]).then_inc(aux_free, 1)
                dve.drain().then_inc(yo_ready, 1)


INS = ["x_prompt", "x_sample", "cache_ckv", "cache_krope", "state_conv", "page_table", "c_prompt", "c_sample",
       "ada_w", "ada_b", "ln_mix_g", "ln_mix_b", "ln_ffn_g", "ln_ffn_b", "ffn_w_gate", "ffn_w_up", "ffn_w_down",
       "gmlp_w_in", "gmlp_ln_g", "gmlp_ln_b", "gmlp_w_s", "gmlp_b_s", "gmlp_w_out",
       "conv_w_pw1", "conv_b_pw1", "conv_w_dw", "conv_b_dw", "conv_ln_g", "conv_ln_b", "conv_w_pw2", "conv_b_pw2",
       "mla_w_down", "mla_g_q", "mla_g_kv", "mla_w_uq", "mla_w_uk", "mla_w_uv", "mla_w_o"]
OUTS_ = {
    "y_prompt": (1, SEQ, D), "y_sample": (DEC_B, DEC_T, D),
    "new_ckv_prompt": (1, 1, SEQ, KVR), "new_krope_prompt": (1, 1, SEQ, ROPE),
    "new_ckv_sample": (1, DEC_B, DEC_T, KVR), "new_krope_sample": (1, DEC_B, DEC_T, ROPE),
    "new_conv_prompt": (1, 1, CTX, D), "new_conv_sample": (1, DEC_B, CTX, D),
    "new_gmlp_v_sample": (2, DEC_B, DEC_T, GDIM),
}


def constants():
    f = np.float32
    q, k = np.arange(P)[:, None], np.arange(P)[None, :]
    causal = np.where(k <= q, 0.0, NEG).astype(f)
    row = np.arange(HEADS * DEC_T) % DEC_T
    col = np.arange(P) - NS
    smask = np.full((HEADS * DEC_T, DEC_B, P), NEG, f)
    for b in range(DEC_B):
        ok = (col[None, :] >= 0) & (col[None, :] // DEC_T == b) & (col[None, :] % DEC_T <= row[:, None])
        smask[:, b][ok] = 0.0
    pos = np.zeros((P, TT), f)
    for t in range(TT - 1):
        pos[:, t] = t * P + np.arange(P)
    pos[:, TT - 1] = np.where(col >= 0, PAST + col % DEC_T, SEQ + col)
    half = ROPE // 2
    inv = (f(10000.0) ** (-np.arange(half, dtype=f) / f(half))).astype(f)
    ang = (pos[:, :, None] * inv).astype(f).astype(np.float64)
    rope = np.concatenate([np.cos(ang), np.sin(ang)], -1).astype(f)
    return {"c_ident": np.eye(P, dtype=f), "c_tril": (k <= q).astype(f), "c_causal": causal,
            "c_smask": smask, "c_rope": rope}


def kernel(**inputs):
    import concourse.bacc as bacc
    from concourse.bass_utils import run_bass_kernel_spmd

    nc = bacc.Bacc("TRN2", target_bir_lowering=False, num_devices=1)
    arrays = {n: np.ascontiguousarray(inputs[n]) for n in INS} | constants()
    feeds, A, O = {}, {}, {}
    for name, a in arrays.items():
        feeds["in_" + name] = a
        A[name] = nc.dram_tensor("in_" + name, a.shape, mybir.dt.from_np(a.dtype), kind="ExternalInput").ap()
    for name, shape in OUTS_.items():
        O[name] = nc.dram_tensor("out_" + name, shape, F32, kind="ExternalOutput").ap()
    trunk(nc, A, O)
    r = run_bass_kernel_spmd(nc, [feeds], core_ids=[0])
    return tuple(r.results[0]["out_" + name] for name in OUTS_)
```

```python
from contextlib import ExitStack, contextmanager

import numpy as np

import concourse.bass as bass
from concourse import mybir

F32 = mybir.dt.float32
F32R = mybir.dt.float32r
I32 = mybir.dt.int32
ACT = mybir.ActivationFunctionType
ALU = mybir.AluOpType
AX = mybir.AxisListType

P = 128
D = 1024
KT = D // P
SEQ = 512
DEC_B, DEC_T = 8, 8
NS = DEC_B * DEC_T
TOK = SEQ + NS
HALF = TOK // 2
HP = SEQ - HALF
TT = 5
DEPTH = 4
NC = 1 + DEC_B
ADA_M = 6 * KT
FFN = 2816
GDIM = 2048
GROUPS = 8
CW = 31
PE_TAPS = 10
CTX = CW - 1
HEADS, NOPE, ROPE, VD = 8, 128, 64, 128
QR, KVR = 384, 256
DOWN = QR + KVR + ROPE
PAGES, PAGE = 8, 128
PAST = PAGES * PAGE
R = HEADS * DEC_T
ALPHA = (2.0 * DEPTH) ** 0.25
LN_EPS, RMS_EPS = 1e-5, 1e-6
SCALE = (NOPE + ROPE) ** -0.5
NEG = -1e30
UNIT = 1024
RAW, SLOTS, BANKS = 2, 4, 4
ADA_RING = 8

C_ADA, C_LN, C_PW1, C_DW, C_CG, C_CB, C_PW2, C_C = 0, 192, 320, 336, 344, 352, 360, 368
C_END = C_C + NC * KT
FULL = CTX + SEQ + DEC_B * (CTX + DEC_T)


class Tally:

    def __init__(self, start=0):
        self.v = start
        self.n = start

    def up(self, k=1):
        self.v = self.v + k
        self.n += k
        return self.v


@contextmanager
def rolled(eng, trips, *steps):
    starts = [(t, s, t.v, t.n) for t, s in steps]
    if trips == 1:
        yield 0
        for t, s, v, n in starts:
            assert t.n == n + s
        return
    with eng.Fori(0, trips) as i:
        for t, s, v, n in starts:
            t.v = i * s + v
        yield i
    for t, s, v, n in starts:
        assert t.n == n + s, (t.n, n, s)
        t.v, t.n = v + trips * s, n + trips * s


N_SETUP = 16
LATE = {0: 5, 2: 6, 3: 7}
OUTS, VOUTS = 3, 8


def SAMPLE_BANK(b, q):
    return BANKS + (7 * b - (b > 0) + q) % BANKS


def token_tile(t):
    return slice(TOK - P, TOK) if t == TT - 1 else slice(t * P, (t + 1) * P)


def half_cols(h):
    return slice(h * HALF, (h + 1) * HALF)


def trunk(nc, A, O):
    ctx = ExitStack()
    with ctx:
        def sem(name):
            return ctx.enter_context(nc.semaphore(name))

        top = [-(-nc.sbuf_base // 64) * 64]

        def at(name, shape, dt, offset):
            return nc.alloc_sbuf_tensor_at(name, shape, dt, offset=offset)

        def size(shape):
            n = 4
            for s in shape[1:]:
                n *= s
            return -(-n // 64) * 64

        def sb(name, shape, dt=F32):
            t = at(name, shape, dt, top[0])
            top[0] += size(shape)
            return t

        def region(nbytes):
            start = top[0]
            top[0] += nbytes
            return start

        class Place:

            def __init__(self, start, nbytes, tag):
                self.at, self.end, self.tag = start, start + nbytes, tag

            def __call__(self, name, shape, dt=F32):
                t = at(name, shape, dt, self.at)
                self.at += size(shape)
                assert self.at <= self.end, (self.tag, name, self.at - self.end)
                return t

        ident = sb("ident", [P, P])
        ones = sb("ones", [P, P])
        xa = sb("xa", [P, KT, TOK])
        par = sb("par", [P, C_END])
        cs = sb("cs", [P, 2 * DEPTH, KT, NC])
        cb = sb("cb", [P, 2 * DEPTH, KT, NC])
        ag = sb("ag", [P, 2 * DEPTH + 1, KT])
        ab = sb("ab", [P, 2 * DEPTH + 1, KT])
        gate = sb("gate", [P, 2 * DEPTH, KT, NC])
        epsl = sb("epsl", [P, 2])
        smt = sb("smt", [P, NS])
        pt_sb = sb("pt_sb", [1, DEC_B * PAGES], I32)
        w_raw = sb("w_raw", [P, RAW, UNIT])
        w_hi = sb("w_hi", [P, SLOTS, UNIT], F32R)
        w_lo = sb("w_lo", [P, SLOTS, UNIT], F32R)
        HB = 2 * KT * TOK * 4
        h_at = region(HB)
        h_hi = at("h_hi", [P, KT, TOK], F32R, h_at)
        h_lo = at("h_lo", [P, KT, TOK], F32R, h_at + HB // 2)
        a_at = region(HB)
        a_hi = at("a_hi", [P, KT, TOK], F32R, a_at)
        a_lo = at("a_lo", [P, KT, TOK], F32R, a_at + HB // 2)
        ada_sb = at("ada_sb", [P, ADA_RING, UNIT], F32, a_at)
        LNB = 4 * TOK * 8
        ln_at = region(LNB)
        lp = Place(ln_at, LNB, "ln")
        s_sum = lp("s_sum", [P, TOK])
        s_sq = lp("s_sq", [P, TOK])
        mean = lp("mean", [P, TOK])
        rstd = lp("rstd", [P, TOK])
        sqt = lp("sqt", [P, 2, HALF])
        hf = lp("hf", [P, 2, HALF])
        sg = lp("sg", [P, 2, HALF])
        pr_at = lp.at
        pr = lp("pr", [P, 2, HALF])
        hfs = at("hfs", [P, KT, NS], F32, pr_at)
        s_at = top[0]
        SB = nc.sbuf_usable_end - s_at

        sp0 = Place(s_at, SB, "setup")
        x_in = sp0("x_in", [P, TT, D])
        stage = sp0("stage", [P, 4, P])
        mod = sp0("mod", [P, ADA_M, NC])
        cact = sp0("cact", [P, NC, KT])
        ada_row = sp0("ada_row", [NC, 2, 512])
        sp1 = Place(s_at, SB, "gmlp")
        v_sb = sp1("v_sb", [P, TT, GDIM])
        wsT = sp1("wsT", [P, GROUPS, P])
        wssT = sp1("wssT", [P, GROUPS, NS])
        bst = sp1("bst", [P, TT, GROUPS, 6])
        bag = sp1("bag", [P, TT, 2])
        vrs = sp1("vrs", [P, TT])
        gl = Place(ln_at, LNB, "gmlp-ln")
        vn = gl("vn", [P, 2, TT, 256])
        u_sb = gl("u_sb", [P, TOK])
        gbt = gl("gbt", [P, 2, 2, 256])
        bsb = gl("bsb", [P, 2, P])
        ga = Place(a_at, HB, "gmlp-act")
        ws_raw = ga("ws_raw", [P, GROUPS, P])
        wss_raw = ga("wss_raw", [NS, GROUPS, P])
        tril = ga("tril", [P, P])
        sp2 = Place(s_at, SB, "conv")
        full = sp2("full", [P, 2, FULL])
        yc = sp2("yc", [P, KT, TOK])
        stT = sp2("stT", [P, KT, DEC_B * CTX])
        snew = sp2("snew", [P, 2, NS])
        wdT = sp2("wdT", [P, KT, CW])
        st_p = sp2("st_p", [CTX, D])
        st_s = sp2("st_s", [NS, D])
        gbw = sp2("gbw", [P, KT, NC])
        ca = Place(a_at, HB, "conv-act")
        wd_in = ca("wd_in", [CW, D])
        prod_at = ca.at
        st_in = ca("st_in", [4 * CTX, 2, D])
        prod = at("prod", [P, DEC_B, DEC_T, CW], F32, prod_at)
        diag = ca("diag", [P, 2, PE_TAPS, P])
        sp3 = Place(s_at, SB, "mla")
        qaT = sp3("qaT", [P, 2, HEADS, TOK])
        qr_at = sp3.at
        qrT = sp3("qrT", [P, HEADS // 2, TOK])
        uv = at("uv", [P, 2, D], F32, qr_at)
        qas = sp3("qas", [P, 2, DEC_B, HEADS, DEC_T])
        ml = Place(ln_at, LNB, "mla-ln")
        ckv = ml("ckv", [P, TT, KVR])
        ckvT = ml("ckvT", [P, 2, TOK])
        krT = ml("krT", [P, TOK])
        kr2 = ml("kr2", [P, TT, 2, ROPE])
        qrs = ml("qrs", [ROPE, DEC_B, HEADS, DEC_T])
        mh = Place(h_at, HB, "mla-h")
        ql_hi = mh("ql_hi", [P, 3, TOK], F32R)
        ql_lo = mh("ql_lo", [P, 3, TOK], F32R)
        ukT = mh("ukT", [P, HEADS, KVR])
        qn = mh("qn", [P, 2, TOK])
        rt = mh("rt", [P, 2, HEADS * ROPE // 2])
        ms = Place(h_at, HB, "mla-h2")
        pg = ms("pg", [P, PAGES, KVR])
        pgr = ms("pgr", [P, PAGES, ROPE])
        pgT = ms("pgT", [P, 2, PAST])
        pgrT = ms("pgrT", [ROPE, PAST])
        pe_at = ms.at
        pexp = ms("pexp", [P, 2, 512])
        pT = ms("pT", [P, 2, 4, P])
        mq = Place(pe_at, 8192, "mla-h3")
        sp_ = mq("sp_", [HEADS * DEC_T, PAST + P])
        spT = mq("spT", [P, PAGES + 1, HEADS * DEC_T])
        scx = at("scx", [HEADS * DEC_T, KVR], F32, mq.at)
        ma = Place(a_at, HB, "mla-act")
        dtok = ma("dtok", [P, TT, DOWN])
        qrt = ma("qrt", [P, TT, HEADS * ROPE])
        ukr = ma("ukr", [P, 2, D])
        rtab = ma("rtab", [P, TT, ROPE])
        gqk = ma("gqk", [P, QR + KVR])
        ssq = ma("ssq", [P, TT, 2])
        mb = Place(a_at, HB, "mla-act2")
        cmask = mb("cmask", [P, P])
        smask = mb("smask", [HEADS * DEC_T, DEC_B, P])
        pg_b = mb("pg_b", [P, PAGES, KVR])
        pgr_b = mb("pgr_b", [P, PAGES, ROPE])
        pgs, pgrs = (pg, pg_b), (pgr, pgr_b)
        att = mb("att", [P, 2, 8])
        satt = mb("satt", [R, 8])
        yo = at("yo", [P, 2, D], F32, s_at)

        pb = ctx.enter_context(nc.psum_tensor("pb", [P, 8, 512], F32))

        const_in = sem("const_in")
        const_made = sem("const_made")
        raw_full = [sem(f"raw_full{i}") for i in range(RAW)]
        ada_full = [sem(f"ada_full{i}") for i in range(ADA_RING)]
        ada_used = sem("ada_used")
        act_c = sem("act_c")
        split_full = sem("split_full")
        split_free = sem("split_free")
        acc_ready = sem("acc_ready")
        acc_free = sem("acc_free")
        aux_ready = sem("aux_ready")
        aux_free = sem("aux_free")
        coef_ready = sem("coef_ready")
        n_ready = sem("n_ready")
        hf_ready = sem("hf_ready")
        h_ready = sem("h_ready")
        xa_ready = sem("xa_ready")
        a_ready = sem("a_ready")
        sq_ready = sem("sq_ready")
        q_done = sem("q_done")
        yc_ready = sem("yc_ready")
        var_ready = sem("var_ready")
        std_ready = sem("std_ready")
        sg_ready = sem("sg_ready")
        v_ready = sem("v_ready")
        ws_in = sem("ws_in")
        ws_zero = sem("ws_zero")
        ws_ready = sem("ws_ready")
        gb_full = [sem(f"gb_full{i}") for i in range(2)]
        vn_ready = sem("vn_ready")
        vo_done = [sem(f"vo_done{i}") for i in range(2)]
        st_in_full = sem("st_in_full")
        full_ready = sem("full_ready")
        wd_ready = sem("wd_ready")
        diag_free = sem("diag_free")
        diag_ready = sem("diag_ready")
        st_ready = sem("st_ready")
        d_ready = sem("d_ready")
        ssq_ready = sem("ssq_ready")
        mla_in = sem("mla_in")
        kv_ready = sem("kv_ready")
        kv_out = sem("kv_out")
        lat_ready = sem("lat_ready")
        qr_ready = sem("qr_ready")
        sc_ready = sem("sc_ready")
        nm_ready = sem("nm_ready")
        sc_free = sem("sc_free")
        p_ready = sem("p_ready")
        pt_ready = sem("pt_ready")
        pt_copied = sem("pt_copied")
        mask_in = sem("mask_in")
        pt_in = sem("pt_in")
        pg_full = [sem(f"pg_full{i}") for i in range(2)]
        pg_used = sem("pg_used")
        se_ready = sem("se_ready")
        uv_full = sem("uv_full")
        yo_ready = sem("yo_ready")
        y_out = [sem(f"y_out{i}") for i in range(2)]
        pool_passed, pe_passed, act_passed = [sem(n + "_passed") for n in ("pool", "pe", "act")]
        out_done = sem("out_done")

        def settle(eng, passed):
            eng.sem_inc(passed, 1)

        def one(t, m, cols=slice(None)):
            if isinstance(m, int):
                return t[:, m, cols]
            return t[:, bass.ds(m, 1), cols].rearrange("p a n -> p (a n)")

        def per_row(t, e, m):
            r = one(t[:, e, :, :], m)
            return r[:, 0:1], r[:, 1:NC].unsqueeze(2).to_broadcast([P, DEC_B, DEC_T])

        def bt(ap):
            return ap.rearrange("p (b t) -> p b t", b=DEC_B)

        def full_s(ap):
            return ap[:, CTX + SEQ:].rearrange("p (b t) -> p b t", b=DEC_B)

        def one1(t, m, off):
            return t[:, off + m:off + m + 1] if isinstance(m, int) else t[:, bass.ds(m + off, 1)]

        def wcols(w, k0, k1, c0, n):
            return w[k0 * P:k1 * P, bass.ds(c0, n)].rearrange("(k p) n -> p k n", p=P)

        GU = ((0, 8), (8, 8), (16, 6))

        def ffn_units(l):
            for first, count in GU:
                yield count // 2, lambda i, first=first: [
                    [wcols(w[l], 0, KT, (i * 2 + (first + mm)) * P, P)]
                    for mm in range(2) for w in (A["ffn_w_gate"], A["ffn_w_up"])]
                yield 2, lambda i, first=first, count=count: [
                    [wcols(A["ffn_w_down"][l], first, first + count, (i * 4 + mm) * P, P)] for mm in range(4)]

        def gmlp_units(j):
            w_in, w_out = A["gmlp_w_in"][j], A["gmlp_w_out"][j]
            yield 2, lambda i: [[wcols(w_in, 4 * kh, 4 * kh + 4, (i * 4 + gg) * 256 + GDIM, 256)]
                                for gg in range(4) for kh in range(2)]
            for ph in range(2):
                yield 2, lambda i, ph=ph: [[wcols(w_in, 0, KT, (i * 4 + (8 * ph + mm)) * P, P)] for mm in range(4)]
                yield 2, lambda i, ph=ph: [[wcols(w_out, 8 * ph, 8 * ph + 8, (i * 4 + mm) * P, P)] for mm in range(4)]

        def conv_units(j):
            yield 4, lambda i: [[wcols(A["conv_w_pw1"][j], 0, KT, (i * 2 + (mm + part * KT)) * P, P)]
                                for mm in range(2) for part in range(2)]
            yield 2, lambda i: [[wcols(A["conv_w_pw2"][j], 0, KT, (i * 4 + mm) * P, P)] for mm in range(4)]

        DCH = ((0, 256), (256, 256), (512, 192))

        def mla_units(j):
            wd, wq = A["mla_w_down"][j], A["mla_w_uq"][j]
            yield 1, lambda i: [[wcols(wd, 4 * kh, 4 * kh + 4, c0, n)] for c0, n in DCH for kh in range(2)]
            wr = wq.rearrange("(k p) (h n) -> k p h n", p=P, h=HEADS)
            yield 1, lambda i: [[wr[k, :, 4 * c:4 * c + 4, NOPE:] for k in range(3)] for c in range(2)]
            yield 1, lambda i: [[wcols(wq, 0, 3, h * (NOPE + ROPE), NOPE)] for h in range(HEADS)]
            yield 2, lambda i: [[wcols(A["mla_w_o"][j], 0, KT, (i * 4 + mm) * P, P)] for mm in range(4)]

        block = ctx.enter_context(nc.Block())

        @block.sync
        def _(sp):
            n_setup = 0
            ada_b = A["ada_b"].rearrange("l (m c) -> (l m) c", c=P)
            loads = [
                (ident[:], A["c_ident"]),
                (stage[:, 0, :], ada_b[0:P]),
                (stage[0:DEPTH * ADA_M - P, 1, :], ada_b[P:]),
            ]
            for n, name in enumerate(("ln_mix_g", "ln_mix_b", "ln_ffn_g", "ln_ffn_b")):
                loads.append((stage[32 * n:32 * n + 32, 2, :], A[name].rearrange("l (m c) -> (l m) c", c=P)))
            row = 0
            for name in ("conv_b_pw1", "conv_b_dw", "conv_ln_g", "conv_ln_b", "conv_b_pw2", "c_prompt", "c_sample"):
                src = A[name].rearrange("l (m c) -> (l m) c", c=P)
                loads.append((stage[row:row + src.shape[0], 3, :], src))
                row += src.shape[0]
            loads.append((x_in[:, 0:4, :], A["x_prompt"][0].rearrange("(t p) d -> p t d", p=P)))
            loads.append((x_in[0:NS, 4, :], A["x_sample"].rearrange("b t d -> (b t) d")))
            for dst, src in loads:
                sp.dma_start(dst, src).then_inc(const_in, 16)
            units = Tally()
            arrived = [Tally(), Tally()]
            ada_u = Tally()
            for l in range(DEPTH):
                with rolled(sp, 6, (ada_u, 8)) as i:
                    for c in range(2):
                        for q in range(4):
                            sp.wait_ge(ada_used, ada_u.v + 1)
                            s = ada_u.n % ADA_RING
                            sp.dma_start(ada_sb[:, s, :].rearrange("p (k n) -> p k n", k=2),
                                         wcols(A["ada_w"][l], 2 * q, 2 * q + 2, i * 1024 + c * 512, 512)
                                         ).then_inc(ada_full[s], 16)
                            ada_u.up()

            def stream(segments, before_unit=None, steps=()):
                for trips, units_of in segments:
                    n = len(units_of(0))
                    per = [0, 0]
                    for u, srcs in enumerate(units_of(0)):
                        per[(units.n + u) % RAW] += 16 * len(srcs)
                    with rolled(sp, trips, (units, n), (arrived[0], per[0]), (arrived[1], per[1]), *steps) as i:
                        for u, srcs in enumerate(units_of(i)):
                            if before_unit:
                                before_unit(i, u)
                            sp.wait_ge(split_full, units.v + 1)
                            s = units.n % RAW
                            at_ = 0
                            for src in srcs:
                                words = src.shape[1] * src.shape[2]
                                sp.dma_start(w_raw[:, s, at_:at_ + words].rearrange(
                                    "p (k n) -> p k n", k=src.shape[1]), src).then_inc(raw_full[s], 16)
                                at_ += words
                            arrived[s].up(16 * len(srcs))
                            units.up()

            gb_n = [0, 0]
            a_n = Tally()
            for l in range(DEPTH):
                j, t = l // 3, 2 * l
                if l % 3 == 0:
                    segs = list(gmlp_units(j))
                    stream(segs[0:1])
                    sp.wait_ge(h_ready, 16 * t + 16)
                    for ph in range(2):
                        def rows(i, u, ph=ph):
                            if u % 2 == 0:
                                par_ = u // 2
                                sp.wait_ge(a_ready, 8 + a_n.v - 4)
                                g = i * 2 + (4 * ph + par_)
                                for n, name in enumerate(("gmlp_ln_g", "gmlp_ln_b")):
                                    sp.dma_start(gbt[:, par_, n, :], A[name][j, bass.ds(g * 256, 256)]
                                                 .partition_broadcast(P)).then_inc(gb_full[par_], 16)
                                sp.dma_start(bsb[:, par_, :], A["gmlp_b_s"][j, bass.ds(g, 1), :]
                                             .broadcast_to([P, P])).then_inc(gb_full[par_], 16)
                                a_n.up(4)
                        stream(segs[1 + 2 * ph:2 + 2 * ph], rows, ((a_n, 8),))
                        stream(segs[2 + 2 * ph:3 + 2 * ph])
                elif l % 3 == 1:
                    stream(conv_units(j))
                    a_n.up(16)
                else:
                    segs = list(mla_units(j))
                    stream(segs[0:3])
                    sp.wait_ge(pt_in, 16)
                    sp.wait_ge(sc_ready, 1)
                    sp.dma_start(cmask[:], A["c_causal"]).then_inc(mask_in, 16)
                    sp.dma_start(smask[:], A["c_smask"]).then_inc(mask_in, 16)
                    for b in range(DEC_B):
                        if b >= 2:
                            sp.wait_ge(pg_used, b - 1)
                        for g in range(PAGES):
                            page = sp.value_load(pt_sb[0:1, b * PAGES + g:b * PAGES + g + 1],
                                                 min_val=0, max_val=A["cache_ckv"].shape[1] - 1)
                            sp.dma_start(pgs[b % 2][:, g, :].unsqueeze(1), A["cache_ckv"][j, bass.ds(page, 1)]
                                         .rearrange("a p c -> p a c")).then_inc(pg_full[b % 2], 16)
                            sp.dma_start(pgrs[b % 2][:, g, :].unsqueeze(1), A["cache_krope"][j, bass.ds(page, 1)]
                                         .rearrange("a p c -> p a c")).then_inc(pg_full[b % 2], 16)
                    sp.wait_ge(pg_used, DEC_B)
                    sp.dma_start(uv[:], A["mla_w_uv"][j].rearrange("(c p) h v -> p c (h v)", p=P)
                                 ).then_inc(uv_full, 16)
                    stream(segs[3:4])
                    a_n.up(16)
                stream(ffn_units(l))
                a_n.up(2 * FFN // P)
            for tt in range(TT):
                sp.wait_ge(yo_ready, tt + 1)
                dst = (O["y_prompt"][0, tt * P:(tt + 1) * P, :] if tt < 4
                       else O["y_sample"].rearrange("b t d -> (b t) d"))
                sp.dma_start(dst, yo[0:dst.shape[0], tt % 2, :]).then_inc(y_out[tt % 2], 16)
            sp.wait_ge(y_out[0], 48)
            sp.wait_ge(y_out[1], 32)
            sp.wait_ge(out_done, OUTS * 16)
            for n in range(2):
                sp.wait_ge(vo_done[n], VOUTS * 16 + 16)
            sp.wait_ge(kv_out, 64)

        @block.gpsimd
        def _(pool):
            pool.sem_inc(split_full, RAW)
            DG = Tally()
            units = Tally()
            arrived = [Tally(), Tally()]
            for l in range(DEPTH):
                segs = list((gmlp_units, conv_units, mla_units)[l % 3](l // 3))
                for trips, units_of in [*segs, *ffn_units(l)]:
                    n = len(units_of(0))
                    per = [0, 0]
                    for u, srcs in enumerate(units_of(0)):
                        per[(units.n + u) % RAW] += 16 * len(srcs)
                    words = [sum(s.shape[1] * s.shape[2] for s in srcs) for srcs in units_of(0)]
                    parts = [len(srcs) for srcs in units_of(0)]
                    taps = l % 3 == 1 and units_of is segs[0][1]
                    if taps:
                        pool.wait_ge(wd_ready, 1)
                    with rolled(pool, trips, (units, n), (arrived[0], per[0]), (arrived[1], per[1]), (DG, 2 * taps)) as i:
                        for w, k in zip(words, parts):
                            s, r = units.n % SLOTS, units.n % RAW
                            arrived[r].up(16 * k)
                            pool.wait_ge(raw_full[r], arrived[r].v)
                            pool.wait_ge(split_free, units.v + 1)
                            settle(pool, pool_passed)
                            nc.gpsimd.tensor_scalar(w_hi[:, s, 0:w], w_raw[:, r, 0:w], 1.0, 1.0, ALU.mult, ALU.mult)
                            pool.drain()
                            nc.gpsimd.tensor_tensor(w_lo[:, s, 0:w], w_raw[:, r, 0:w],
                                                    w_hi[:, s, 0:w].bitcast(F32), ALU.subtract
                                                    ).then_inc(split_full, 1)
                            units.up()
                        for m in range(2 if taps else 0):
                            pool.wait_ge(diag_free, DG.up())
                            settle(pool, pool_passed)
                            nc.gpsimd.tensor_tensor(
                                diag[:, m], ident[:].unsqueeze(1).to_broadcast([P, PE_TAPS, P]),
                                one(wdT, i * 2 + m, slice(0, PE_TAPS)).unsqueeze(2).to_broadcast([P, PE_TAPS, P]),
                                ALU.mult).then_inc(diag_ready, 1)

        @block.tensor
        def _(pe):
            pe.sem_inc(ada_used, ADA_RING)
            pe.sem_inc(split_free, SLOTS)
            pe.sem_inc(diag_free, 2)
            U, G, X, AR = Tally(), Tally(), Tally(), Tally()

            def take_units(k):
                pe.wait_ge(split_full, U.v + k + RAW)
                slots = [(U.n + n) % SLOTS for n in range(k)]
                U.up(k)
                return slots

            def mm(out, lhsT, rhs, start, stop):
                return nc.tensor.matmul(out, lhsT, rhs, start=start, stop=stop)

            def acc_bank():
                pe.wait_ge(acc_free, G.v + 1)
                return G.n % BANKS

            def aux_bank():
                pe.wait_ge(aux_free, X.v + 1)
                return BANKS + X.n % BANKS

            def product(out, ks, w_at, m_hi, m_lo, w_moves=False):
                n = len(ks)
                for q, k in enumerate(ks):
                    s, cols = w_at(k)
                    wh, wl = w_hi[:, s, cols], w_lo[:, s, cols]
                    ah, al = m_hi(k), m_lo(k)
                    for e, (w, a) in enumerate(((wh, ah), (wh, al), (wl, ah))):
                        lhsT, rhs = (a, w) if w_moves else (w, a)
                        last = mm(out, lhsT, rhs, q == 0 and e == 0, q == n - 1 and e == 2)
                return last

            def half_product(slot, kt, h, act, waits=None):
                b = acc_bank()
                hi, lo = act
                if waits is not None:
                    for k in range(kt):
                        pe.wait_ge(h_ready, waits + 8 * h + k + 1)
                        for e, (w, a) in enumerate(((w_hi, hi), (w_hi, lo), (w_lo, hi))):
                            last = mm(pb[:, b, 0:HALF], w[:, slot, k * P:(k + 1) * P], a[:, k, half_cols(h)],
                                      k == 0 and e == 0, k == kt - 1 and e == 2)
                else:
                    last = product(pb[:, b, 0:HALF], range(kt), lambda k: (slot, slice(k * P, (k + 1) * P)),
                                   lambda k: hi[:, k, half_cols(h)], lambda k: lo[:, k, half_cols(h)])
                last.then_inc(acc_ready, 1)
                G.up()

            def transposes(parts):
                b = aux_bank()
                settle(pe, pe_passed)
                for n, (c0, src) in enumerate(parts):
                    rows, cols = src.shape
                    last = nc.tensor.transpose(pb[0:cols, b, c0:c0 + rows], src, ident[0:rows, 0:rows])
                last.then_inc(aux_ready, 1)
                X.up()

            def down(kt):
                with rolled(pe, 2, (U, 4), (G, 8)):
                    for mm_ in range(4):
                        (s,) = take_units(1)
                        for h in range(2):
                            pe.wait_ge(a_ready, 8 + AR.v - 1 + h)
                            half_product(s, kt, h, (a_hi, a_lo))

            def half_stats(h, squares):
                pe.wait_ge(q_done, 2 + QD.v + squares)
                for src in (s_sum, s_sq):
                    b = aux_bank()
                    mm(pb[:, b, 0:HALF], ones[:], src[:, half_cols(h)], True, True).then_inc(aux_ready, 1)
                    X.up()

            def down_norm(kt):
                for m in range(4):
                    (s,) = take_units(1)
                    for h in range(2):
                        pe.wait_ge(a_ready, 8 + AR.v - 1 + h)
                        half_product(s, kt, h, (a_hi, a_lo))
                slots = []
                for m in range(4):
                    slots += take_units(1)
                    half_product(slots[m], kt, 0, (a_hi, a_lo))
                for m in range(4):
                    half_product(slots[m], kt, 1, (a_hi, a_lo))
                    if m == 0:
                        half_stats(0, 12)
                half_stats(1, 16)
                QD.up(16)

            QD = Tally()

            def gate_up(count, wait_h, fresh):
                if fresh:
                    slots = take_units(4)
                    for h in range(2):
                        for m in range(2):
                            for s in slots[2 * m:2 * m + 2]:
                                half_product(s, KT, h, (h_hi, h_lo), wait_h)
                with rolled(pe, count // 2 - fresh, (U, 4), (G, 8)):
                    for m in range(2):
                        s_a, s_b = take_units(2)
                        for h in range(2):
                            for s in (s_a, s_b):
                                half_product(s, KT, h, (h_hi, h_lo))

            pe.wait_ge(const_in, 16 * N_SETUP)
            pe.wait_ge(const_made, 1)
            for n, rows in enumerate((P, DEPTH * ADA_M - P, P, C_END - C_PW1)):
                transposes([(0, stage[0:rows, n, :])])
            for tt in range(TT):
                rows = P if tt < 4 else NS
                for q in range(2):
                    transposes([(i * P, x_in[0:rows, tt, (4 * q + i) * P:(4 * q + i + 1) * P]) for i in range(4)])
            pe.wait_ge(act_c, 1)
            ada_u, ada_in = Tally(), Tally()
            for l in range(DEPTH):
                with rolled(pe, 6, (ada_u, 8), (X, 4), (ada_in, 16)):
                    ada_in.v = ada_in.v + 16
                    ada_in.n += 16
                    rows = X.v + BANKS
                    for c in range(2):
                        b = aux_bank()
                        for q in range(4):
                            s = ada_u.n % ADA_RING
                            pe.wait_ge(ada_full[s], ada_in.v)
                            for k in range(2):
                                last = mm(pb[0:NC, b, :], cact[:, :, 2 * q + k],
                                          ada_sb[:, s, k * 512:(k + 1) * 512], q == 0 and k == 0, q == 3 and k == 1)
                            if q < 3:
                                last.then_inc(ada_used, 1)
                            ada_u.up()
                        last.then_inc(aux_ready, 1)
                        pe.drain().then_inc(ada_used, 1)
                        X.up()
                    for c in range(2):
                        pe.wait_ge(aux_free, rows + c + 1)
                        b = aux_bank()
                        settle(pe, pe_passed)
                        for i in range(4):
                            last = nc.tensor.transpose(pb[:, b, i * NC:(i + 1) * NC], ada_row[:, c, i * P:(i + 1) * P],
                                                       ident[0:NC, 0:NC])
                        last.then_inc(aux_ready, 1)
                        X.up()

            def gmlp(l):
                t = 2 * l
                with rolled(pe, 2, (U, 8), (G, 20)):
                    for gg in range(4):
                        slots = take_units(2)
                        for tt in range(TT):
                            pe.wait_ge(h_ready, 16 * t + (8 if tt < 2 else 16))
                            b = acc_bank()
                            product(pb[:, b, 0:256], range(KT),
                                    lambda k: (slots[k // 4], slice(k % 4 * 256, k % 4 * 256 + 256)),
                                    lambda k: h_hi[:, k, token_tile(tt)], lambda k: h_lo[:, k, token_tile(tt)],
                                    w_moves=True).then_inc(acc_ready, 1)
                            G.up()
                pe.wait_ge(ws_ready, l // 3 + 1)
                for q in range(2):
                    transposes([(i * P, ws_raw[:, 4 * q + i, :]) for i in range(4)])
                transposes([(g * NS, wss_raw[:, g, :]) for g in range(GROUPS)])
                for ph in range(2):
                    with rolled(pe, 2, (U, 4), (G, 8), (X, 8), (VN, 2)) as i:
                        for gg in range(2):
                            g = i * 2 + (4 * ph + gg)
                            VN.up()
                            for mt in range(2):
                                (s,) = take_units(1)
                                for h in range(2):
                                    half_product(s, KT, h, (h_hi, h_lo))
                                pe.wait_ge(vn_ready, VN.v)
                                b = aux_bank()
                                for tt in range(4):
                                    last = mm(pb[:, b, tt * P:(tt + 1) * P], vn[:, gg, tt, mt * P:(mt + 1) * P],
                                              one(wsT, g), True, True)
                                last.then_inc(aux_ready, 1)
                                X.up()
                                b = aux_bank()
                                mm(pb[:, b, 0:NS], vn[:, gg, 4, mt * P:(mt + 1) * P], one(wssT, g),
                                   True, True).then_inc(aux_ready, 1)
                                X.up()
                    AR.up(16)
                    if ph == 0:
                        down(KT)
                down_norm(KT)

            VN = Tally()

            def conv(l):
                t = 2 * l
                pe.wait_ge(st_in_full, 48)
                transposes([(k * CW, wd_in[:, k * P:(k + 1) * P]) for k in range(KT)])
                for k in range(KT):
                    transposes([(n * 4 * CTX, st_in[:, n, k * P:(k + 1) * P]) for n in range(2)])
                FR = Tally()
                with rolled(pe, 4, (U, 4), (G, 8), (X, 4), (FR, 2)):
                    for m in range(2):
                        s_a, s_b = take_units(2)
                        for h in range(2):
                            for s in (s_a, s_b):
                                half_product(s, KT, h, (h_hi, h_lo), 16 * t)
                    for m in range(2):
                        pe.wait_ge(diag_ready, FR.v + 1)
                        pe.wait_ge(full_ready, FR.up())
                        b = aux_bank()
                        for k in range(PE_TAPS):
                            last = mm(pb[:, b, :], diag[:, m, k, :], full[:, m, k:k + SEQ], k == 0, k == PE_TAPS - 1)
                        last.then_inc(aux_ready, 1)
                        X.up()
                        pe.drain().then_inc(diag_free, 1)
                        transposes([(0, full[:, m, SEQ:SEQ + CTX]), (P, snew[:, m, :])])
                for h in range(2):
                    half_stats(h, 15 + h)
                QD.up(16)
                AR.up(16)
                down_norm(KT)

            def tok_major(chunks, kts, hi, lo, waits):
                for slots_of, n, nslots in chunks:
                    slots = take_units(nslots)
                    for tt in range(TT):
                        if waits is not None:
                            pe.wait_ge(h_ready, waits + (8 if tt < 2 else 16))
                        b = acc_bank()
                        product(pb[:, b, 0:n], range(kts),
                                lambda k: (slots[slots_of(k)[0]], slice(slots_of(k)[1] * n, (slots_of(k)[1] + 1) * n)),
                                lambda k: hi[:, k, token_tile(tt)], lambda k: lo[:, k, token_tile(tt)],
                                w_moves=True).then_inc(acc_ready, 1)
                        G.up()

            def mla(l):
                t = 2 * l
                tok_major([(lambda k: (k // 4, k % 4), n, 2) for _, n in DCH], KT, h_hi, h_lo, 16 * t)
                pe.wait_ge(mla_in, 64)
                for q in range(4):
                    transposes([((hh * 2 + c) * P, ukr[:, c, (2 * q + hh) * P:(2 * q + hh + 1) * P])
                                for hh in range(2) for c in range(2)])
                pe.wait_ge(kv_ready, 1)
                for k in range(6):
                    def src(tt):
                        if k < 3:
                            return dtok[:, tt, k * P:(k + 1) * P]
                        return ckv[:, tt, (k - 3) * P:(k - 2) * P] if k < 5 else kr2[:, tt, :, :].rearrange("p a n -> p (a n)")
                    transposes([(tt * P, src(tt)) for tt in range(4)])
                    transposes([(0, src(4))])
                pe.wait_ge(lat_ready, 1)
                tok_major([(lambda k: (0, k), 256, 1)] * 2, 3, ql_hi, ql_lo, None)
                def absorb(h):
                    pe.wait_ge(acc_free, BANKS + nope_done[h])
                    for c in range(2):
                        for hf_ in range(2):
                            b = acc_bank()
                            mm(pb[:, b, 0:HALF], ukT[:, h, c * P:(c + 1) * P], qn[:, h % 2, half_cols(hf_)],
                               True, True).then_inc(acc_ready, 1)
                            G.up()
                nope_done = {}
                for h in range(HEADS):
                    (s,) = take_units(1)
                    for hf_ in range(2):
                        half_product(s, 3, hf_, (ql_hi, ql_lo))
                    nope_done[h] = G.v
                    if h:
                        absorb(h - 1)
                absorb(HEADS - 1)
                pe.wait_ge(qr_ready, 1)
                for q in range(4):
                    transposes([(tt * P, qrt[:, tt, q * P:(q + 1) * P]) for tt in range(4)])
                    transposes([(0, qrt[:, 4, q * P:(q + 1) * P])])
                for q in range(2):
                    transposes([(i * P, qrt[:, 4, (4 * q + i) * ROPE:(4 * q + i + 1) * ROPE]) for i in range(4)])
                pe.wait_ge(acc_free, G.v + BANKS)
                pe.wait_ge(aux_free, X.v + BANKS)
                def scores(n):
                    qb, h = divmod(n, HEADS)
                    N, q = (qb + 1) * P, slice(qb * P, (qb + 1) * P)
                    if n >= 2:
                        pe.wait_ge(sc_free, n - 1)
                    o = pb[:, 4 + n % 2, 0:N]
                    r = slice(h % 2 * ROPE, (h % 2 + 1) * ROPE)
                    for c in range(2):
                        mm(o, qaT[:, c, h, q], ckvT[:, c, 0:N], c == 0, False)
                    mm(o, qrT[r, h // 2, q], krT[r, 0:N], False, True).then_inc(sc_ready, 1)

                def contexts(n):
                    qb, h = divmod(n, HEADS)
                    pe.wait_ge(pt_copied, n + 1)
                    b = acc_bank()
                    for c in range(2):
                        for kb in range(qb + 1):
                            last = mm(pb[:, b, c * P:(c + 1) * P], ckv[:, kb, c * P:(c + 1) * P], pT[:, n % 2, kb, :],
                                      kb == 0, kb == qb)
                    last.then_inc(acc_ready, 1)
                    G.up()

                NA = 4 * HEADS
                scores(0)
                scores(1)
                for n in range(NA):
                    pe.wait_ge(p_ready, n + 1)
                    if n >= 2:
                        pe.wait_ge(pt_copied, n - 1)
                    for kb in range(n // HEADS + 1):
                        last = nc.tensor.transpose(pb[:, 6 + n % 2, kb * P:(kb + 1) * P],
                                                   pexp[:, n % 2, kb * P:(kb + 1) * P], ident[:])
                    last.then_inc(pt_ready, 1)
                    if n + 2 < NA:
                        scores(n + 2)
                    contexts(n)
                pe.wait_ge(sc_free, NA)
                pe.wait_ge(pt_copied, NA)
                def turn_pages(b_):
                    pe.wait_ge(pg_full[b_ % 2], 16 * 16 * (b_ // 2 + 1))
                    parts = [(pgs[b_ % 2], c * P, P, q) for c in range(2) for q in range(2)]
                    for t_, c0, n, q in parts + [(pgrs[b_ % 2], 0, ROPE, q) for q in range(2)]:
                        b = acc_bank()
                        for i in range(4):
                            last = nc.tensor.transpose(pb[0:n, b, i * P:(i + 1) * P], t_[:, 4 * q + i, c0:c0 + n],
                                                       ident[:])
                        last.then_inc(acc_ready, 1)
                        G.up()

                turn_pages(0)
                for b_ in range(DEC_B):
                    pe.wait_ge(acc_free, G.v + BANKS)
                    for q in range(3):
                        k0, k1 = (q * 512, (q + 1) * 512) if q < 2 else (TOK - P, TOK)
                        kc, kr_ = (pgT, pgrT) if q < 2 else (ckvT, krT)
                        b = aux_bank()
                        o = pb[0:R, b, 0:k1 - k0]
                        for c in range(2):
                            mm(o, qas[:, c, b_].rearrange("p h t -> p (h t)"), kc[:, c, k0:k1], c == 0, False)
                        mm(o, qrs[:, b_].rearrange("p h t -> p (h t)"), kr_[0:ROPE, k0:k1], False, True
                           ).then_inc(aux_ready, 1)
                        X.up()
                    if b_ + 1 < DEC_B:
                        turn_pages(b_ + 1)
                    if b_:
                        pe.wait_ge(aux_free, context)
                        transposes([(c * R, scx[:, c * P:(c + 1) * P]) for c in range(2)])
                    pe.wait_ge(aux_free, X.v + BANKS - (1 if b_ else 0))
                    transposes([(g * R, sp_[:, g * P:(g + 1) * P]) for g in range(8)])
                    transposes([(0, sp_[:, PAST:])])
                    pe.wait_ge(aux_free, X.v + BANKS)
                    b = aux_bank()
                    for g in range(PAGES + 1):
                        last = mm(pb[0:R, b, 0:KVR], spT[:, g, :], pgs[b_ % 2][:, g, :] if g < PAGES else ckv[:, 4, :],
                                  g == 0, g == PAGES)
                    last.then_inc(aux_ready, 1)
                    X.up()
                    context = X.v + BANKS
                pe.wait_ge(aux_free, context)
                transposes([(c * R, scx[:, c * P:(c + 1) * P]) for c in range(2)])
                pe.wait_ge(aux_free, X.v + BANKS)
                pe.wait_ge(acc_free, G.v + BANKS)
                pe.wait_ge(uv_full, 16)
                for h in range(HEADS):
                    for hf_ in range(2):
                        b = acc_bank()
                        for c in range(2):
                            last = mm(pb[:, b, 0:HALF], uv[:, c, h * P:(h + 1) * P], qaT[:, c, h, half_cols(hf_)],
                                      c == 0, c == 1)
                        last.then_inc(acc_ready, 1)
                        G.up()
                AR.up(16)
                down_norm(KT)

            for l in range(DEPTH):
                (gmlp, conv, mla)[l % 3](l)
                for n, (first, count) in enumerate(GU):
                    gate_up(count, 16 * (2 * l + 1), n == 0)
                    AR.up(2 * count)
                    if n < 2:
                        down(count)
                down_norm(GU[2][1])
            pe.wait_ge(xa_ready, 16 * (2 * DEPTH + 1))
            for tt in range(TT):
                cols = slice(tt * P, min((tt + 1) * P, TOK))
                for q in range(2):
                    b = aux_bank()
                    for i in range(4):
                        last = nc.tensor.transpose(pb[0:cols.stop - cols.start, b, i * P:(i + 1) * P],
                                                   xa[:, 4 * q + i, cols], ident[:])
                    last.then_inc(aux_ready, 1)
                    X.up()

        @block.scalar
        def _(act):
            fn = nc.scalar.activation
            G, Q, SV, VNA, KA = Tally(), Tally(), Tally(), Tally(), Tally()

            act.wait_ge(coef_ready, 1)
            fn(cact[:].rearrange("p n k -> p (n k)"), par[:, C_C:C_END], ACT.Silu).then_inc(act_c, 1)
            act.wait_ge(coef_ready, 2)

            def square(m, h):
                act.wait_ge(acc_free, G.v + 1 + BANKS)
                act.wait_ge(q_done, Q.v + 2)
                fn(sqt[:, h, :], xa[:, m, half_cols(h)], ACT.Square).then_inc(sq_ready, 1)
                G.up()
                Q.up()

            def down_norm():
                for m in range(4):
                    for h in range(2):
                        square(m, h)
                for m in range(4, KT):
                    square(m, 0)
                square(4, 1)

            def apply(t):
                for h in range(2):
                    if t:
                        act.wait_ge(var_ready, SV.up())
                        fn(rstd[:, half_cols(h)], rstd[:, half_cols(h)], ACT.Sqrt, bias=epsl[:, 0:1]
                           ).then_inc(std_ready, 1)
                    n = 16 * t + 8 * h

                    w = HALF if h == 0 else HP
                    for m in range(KT):
                        if t and h == 0 and m in LATE:
                            square(LATE[m], 1)
                        act.wait_ge(n_ready, n + m + 1)
                        if n + m >= 2:
                            act.wait_ge(h_ready, n + m - 1)
                        for dst in (hf[:, m % 2, 0:w], h_hi[:, m, h * HALF:h * HALF + w]):
                            last = fn(dst, xa[:, m, h * HALF:h * HALF + w], ACT.Identity,
                                      scale=cs[:, t, m, 0:1], bias=cb[:, t, m, 0:1])
                        last.then_inc(hf_ready, 1)

            def residuals(t):
                act.wait_ge(h_ready, 16 * (t + 1))
                for h in range(2):
                    for m in range(KT):
                        fn(xa[:, m, half_cols(h)], xa[:, m, half_cols(h)], ACT.Identity,
                           scale=ag[:, t, m:m + 1], bias=ab[:, t, m:m + 1]).then_inc(xa_ready, 1)

            def final():
                t = 2 * DEPTH
                for h in range(2):
                    act.wait_ge(var_ready, SV.up())
                    fn(rstd[:, half_cols(h)], rstd[:, half_cols(h)], ACT.Sqrt, bias=epsl[:, 0:1]
                       ).then_inc(std_ready, 1)
                    for m in range(KT):
                        if h == 0 and m in LATE:
                            square(LATE[m], 1)
                        act.wait_ge(n_ready, 16 * t + 8 * h + m + 1)
                        fn(xa[:, m, half_cols(h)], xa[:, m, half_cols(h)], ACT.Identity,
                           scale=ag[:, t, m:m + 1], bias=ab[:, t, m:m + 1]).then_inc(xa_ready, 1)

            def gate(q, b, func, **kw):
                act.wait_ge(acc_free, G.v - 2 + BANKS)
                act.wait_ge(acc_ready, G.v + 1)
                fn(sg[:, q, :], pb[:, b, 0:HALF], func, **kw).then_inc(sg_ready, 1)
                G.up(2)

            def ffn_gates(count, t):
                fresh = t is not None
                if fresh:
                    for q in range(4):
                        gate(q % 2, G.n % BANKS, ACT.Silu)
                    residuals(t)
                with rolled(act, count // 2 - fresh, (G, 8)):
                    for q in range(4):
                        gate(q % 2, G.n % BANKS, ACT.Silu)

            def gates(trips, func, bias=None, after=None, steps=()):
                with rolled(act, trips, (G, 8), *steps) as i:
                    for m in range(2):
                        for h in range(2):
                            act.wait_ge(acc_free, G.v - 2 + BANKS)
                            g = G.v + (1 if bias is None else 2)
                            act.wait_ge(acc_ready, g)
                            if bias is not None:
                                settle(act, act_passed)
                            b = (G.n + (0 if bias is None else 1)) % BANKS
                            kw = {} if bias is None else {"bias": bias(i * 2 + m)}
                            fn(sg[:, h, :], pb[:, b, 0:HALF], func, **kw).then_inc(sg_ready, 1)
                            G.up(2)
                    if after:
                        after(i)

            def gmlp(l):
                j, ws = l // 3, A["gmlp_w_s"][l // 3]
                act.wait_ge(ws_zero, j + 1)
                act.dma_start(ws_raw[:], ws.rearrange("g t s -> t g s")).then_inc(ws_in, 16)
                act.dma_start(tril[:], A["c_tril"]).then_inc(ws_in, 16)
                for b in range(DEC_B):
                    act.dma_start(wss_raw[8 * b:8 * b + 8, :, NS + 8 * b:NS + 8 * b + 8],
                                  ws[:, 0:8, 0:8].rearrange("g t s -> t g s")).then_inc(ws_in, 16)
                residuals(2 * l)
                with rolled(act, 2, (G, 20)) as i:
                    for gg in range(4):
                        for tt in range(TT):
                            act.wait_ge(acc_ready, G.v + 1)
                            settle(act, act_passed)
                            fn(v_sb[:, tt, bass.ds(i * 1024 + gg * 256, 256)], pb[:, G.n % BANKS, 0:256], ACT.Gelu
                               ).then_inc(v_ready, 1)
                            G.up()
                act.wait_ge(var_ready, SV.up())
                fn(vrs[:], bag[:, :, 1], ACT.Sqrt, bias=epsl[:, 0:1]).then_inc(std_ready, 1)
                for ph in range(2):
                    with rolled(act, 2, (G, 8), (KA, 8), (VNA, 2)) as i:
                        for gg in range(2):
                            act.wait_ge(vn_ready, VNA.up())
                            act.dma_start(O["new_gmlp_v_sample"][l // 3].rearrange("b t c -> (b t) c")
                                          [:, bass.ds((i * 2 + (4 * ph + gg)) * 256, 256)],
                                          vn[NS:P, gg, 4, :]).then_inc(vo_done[gg], 16)
                            for mt in range(2):
                                for h in range(2):
                                    act.wait_ge(acc_ready, G.v + 1)
                                    act.wait_ge(a_ready, KA.v + 7)
                                    fn(u_sb[:, half_cols(h)], pb[:, G.n % BANKS, 0:HALF], ACT.Gelu
                                       ).then_inc(sg_ready, 1)
                                    G.up()
                                    KA.up()
                    if ph == 0:
                        G.up(16)
                down_norm()

            def conv(l):
                j = l // 3
                st = A["state_conv"][j].rearrange("b r d -> (b r) d")
                for n in range(2):
                    act.dma_start(st_in[:, n, :], st[n * 4 * CTX:(n + 1) * 4 * CTX]).then_inc(st_in_full, 16)
                act.dma_start(wd_in[:], A["conv_w_dw"][j]).then_inc(st_in_full, 16)
                act.dma_start(O["new_conv_sample"][j, :, 0:CTX - DEC_T, :],
                              A["state_conv"][j, :, DEC_T:, :]).then_inc(out_done, 16)
                residuals(2 * l)
                YC = Tally()

                def squares(i):
                    for m in range(2):
                        act.wait_ge(yc_ready, YC.up())
                        for h in range(2):
                            act.wait_ge(q_done, Q.v + 1)
                            settle(act, act_passed)
                            fn(sqt[:, h, :], one(yc, i * 2 + m, half_cols(h)), ACT.Square).then_inc(sq_ready, 1)
                            Q.up()

                gates(4, ACT.Sigmoid, lambda j: one1(par, j, C_PW1 + KT), squares, ((Q, 4), (YC, 2)))
                act.wait_ge(st_ready, 1)
                act.dma_start(O["new_conv_prompt"][0, 0], st_p[:]).then_inc(out_done, 16)
                act.dma_start(O["new_conv_sample"][0, :, CTX - DEC_T:, :], st_s[:]).then_inc(out_done, 16)
                for h in range(2):
                    act.wait_ge(var_ready, SV.up())
                    fn(rstd[:, half_cols(h)], rstd[:, half_cols(h)], ACT.Sqrt, bias=epsl[:, 0:1]
                       ).then_inc(std_ready, 1)
                    for m in range(KT):
                        act.wait_ge(yc_ready, KT + 8 * h + m + 1)
                        act.wait_ge(a_ready, KA.v + 8 - 1)
                        for dst in (hf[:, m % 2, :], a_hi[:, m, half_cols(h)]):
                            last = fn(dst, yc[:, m, half_cols(h)], ACT.Silu, scale=par[:, C_CG + m:C_CG + m + 1],
                                      bias=par[:, C_CB + m:C_CB + m + 1])
                        last.then_inc(hf_ready, 1)
                        KA.up()
                down_norm()

            def mla(l):
                j = l // 3
                act.dma_start(rtab[:], A["c_rope"]).then_inc(mla_in, 16)
                act.dma_start(gqk[:, 0:QR], A["mla_g_q"][j].partition_broadcast(P)).then_inc(mla_in, 16)
                act.dma_start(gqk[:, QR:], A["mla_g_kv"][j].partition_broadcast(P)).then_inc(mla_in, 16)
                act.dma_start(ukr[:], A["mla_w_uk"][j].rearrange("(c p) h n -> p c (h n)", p=P)
                              ).then_inc(mla_in, 16)
                act.dma_start(pt_sb[:], A["page_table"].rearrange("b g -> (b g)").unsqueeze(0)
                              ).then_inc(pt_in, 16)
                residuals(2 * l)
                G.up(15)
                act.wait_ge(d_ready, 1)
                act.wait_ge(out_done, OUTS * 16)
                for tt in range(TT):
                    fn(qaT[:, 1, tt, 0:QR], dtok[:, tt, 0:QR], ACT.Square, accum_out=ssq[:, tt, 0:1])
                    fn(qaT[:, 0, tt, 0:KVR], dtok[:, tt, QR:QR + KVR], ACT.Square, accum_out=ssq[:, tt, 1:2])
                act.drain()
                for n, width in enumerate((QR, KVR)):
                    last = fn(ssq[:, :, n], ssq[:, :, n], ACT.Sqrt, scale=1.0 / width, bias=epsl[:, 1:2])
                last.then_inc(ssq_ready, 1)
                act.wait_ge(kv_ready, 1)
                o_ckv, o_kr = O["new_ckv_prompt"][0, 0], O["new_krope_prompt"][0, 0]
                act.dma_start(o_ckv.rearrange("(t p) c -> p t c", p=P), ckv[:, 0:4, :]).then_inc(kv_out, 16)
                act.dma_start(o_kr.rearrange("(t p) c -> p t c", p=P), kr2[:, 0:4, 0, :]).then_inc(kv_out, 16)
                act.dma_start(O["new_ckv_sample"][0].rearrange("b t c -> (b t) c"), ckv[NS:P, 4, :]
                              ).then_inc(kv_out, 16)
                act.dma_start(O["new_krope_sample"][0].rearrange("b t c -> (b t) c"), kr2[NS:P, 4, 0, :]
                              ).then_inc(kv_out, 16)
                G.up(10 + 6 * HEADS)
                NA = 4 * HEADS

                def expo(n):
                    N = (n // HEADS + 1) * P
                    act.wait_ge(nm_ready, n + 1)
                    if n >= 2:
                        act.wait_ge(pt_ready, n - 1)
                    fn(pexp[:, n % 2, 0:N], pb[:, 4 + n % 2, 0:N], ACT.Exp, scale=SCALE, bias=att[:, n % 2, 0:1],
                       accum_out=att[:, n % 2, 1:2])
                    act.drain().then_inc(sc_free, 1)

                expo(0)
                for n in range(NA):
                    if n + 1 < NA:
                        expo(n + 1)
                    N = (n // HEADS + 1) * P
                    act.wait_ge(pt_ready, n + 1)
                    if n >= 2:
                        act.wait_ge(acc_ready, G.v - 1)
                    fn(pT[:, n % 2, :, :].rearrange("p k q -> p (k q)")[:, 0:N], pb[:, 6 + n % 2, 0:N], ACT.Copy
                       ).then_inc(pt_copied, 1)
                    G.up()
                for b in range(DEC_B):
                    act.wait_ge(nm_ready, NA + b + 1)
                    for q in range(3):
                        k0, k1 = (q * 512, (q + 1) * 512) if q < 2 else (PAST, PAST + P)
                        fn(sp_[:, k0:k1], pb[0:R, SAMPLE_BANK(b, q), 0:k1 - k0], ACT.Exp, scale=SCALE,
                           bias=satt[:, 0:1], accum_out=satt[:, 1 + q:2 + q])
                    act.drain().then_inc(se_ready, 1)
                G.up(6 * DEC_B + 2 * HEADS)
                KA.up(16)
                down_norm()

            apply(0)
            for l in range(DEPTH):
                (gmlp, conv, mla)[l % 3](l)
                apply(2 * l + 1)
                for n, (first, count) in enumerate(GU):
                    ffn_gates(count, None if n else 2 * l + 1)
                    KA.up(2 * count)
                    if n < 2:
                        G.up(16)
                down_norm()
                if l < DEPTH - 1:
                    apply(2 * l + 2)
                else:
                    final()

        @block.vector
        def _(dve):
            v = nc.vector
            G, X, SG = Tally(), Tally(), Tally()
            ST, SQ, GB = Tally(), Tally(), [Tally(), Tally()]

            def aux():
                dve.wait_ge(aux_ready, X.v + 1)
                b = BANKS + X.n % BANKS
                X.up()
                return b

            def split(hi, lo, src):
                v.tensor_copy(hi, src)
                dve.drain()
                return v.tensor_tensor(lo, src, hi.bitcast(F32), ALU.subtract)

            dve.sem_inc(acc_free, BANKS)
            dve.sem_inc(aux_free, BANKS)
            dve.sem_inc(a_ready, 8)
            dve.sem_inc(q_done, 2)
            for n in range(2):
                dve.sem_inc(vo_done[n], 16)
            v.memset(ones[:], 1.0 / D)
            v.memset(epsl[:, 0:1], LN_EPS)
            v.memset(epsl[:, 1:2], RMS_EPS)
            dve.drain().then_inc(const_made, 1)
            for c0, rows in ((C_ADA, P), (C_ADA + P, DEPTH * ADA_M - P), (C_LN, P), (C_PW1, C_END - C_PW1)):
                v.tensor_copy(par[:, c0:c0 + rows], pb[:, aux(), 0:rows]).then_inc(aux_free, 1)
            dve.drain().then_inc(coef_ready, 1)
            for tt in range(TT):
                n = P if tt < 4 else NS
                for q in range(2):
                    v.tensor_copy(xa[:, 4 * q:4 * q + 4, tt * P:tt * P + n],
                                  pb[:, aux(), :].rearrange("p (m t) -> p m t", m=4)[:, :, 0:n]
                                  ).then_inc(aux_free, 1)
            v.memset(ag[:, 0, :], ALPHA)
            v.memset(ab[:, 0, :], 0.0)

            def ln_rows(kind, l):
                c0 = C_LN + 32 * kind + KT * l
                return par[:, c0:c0 + KT]

            def modulation(l):
                with rolled(dve, 6, (X, 4)) as i:
                    for c in range(2):
                        v.tensor_copy(ada_row[:, c, :], pb[0:NC, aux(), :]).then_inc(aux_free, 1)
                    for c in range(2):
                        b = aux()
                        v.tensor_tensor(mod[:, bass.ds(i * 8 + c * 4, 4), :],
                                        pb[:, b, 0:4 * NC].rearrange("p (m n) -> p m n", m=4),
                                        par[:, bass.ds(i * 8 + (c * 4 + ADA_M * l), 4)].unsqueeze(2)
                                        .to_broadcast([P, 4, NC]), ALU.add).then_inc(aux_free, 1)
                dve.drain()
                part = [mod[:, KT * n:KT * (n + 1), :] for n in range(6)]
                for n in range(2):
                    t = 2 * l + n
                    shift, scale, g = part[3 * n:3 * n + 3]
                    v.tensor_copy(gate[:, t], g)
                    if t:
                        gain, bias = [ln_rows(2 * (1 - n) + e, l - 1 + n).unsqueeze(2).to_broadcast([P, KT, NC])
                                      for e in range(2)]
                        v.scalar_tensor_tensor(out=cs[:, t], in0=scale, scalar=1.0, in1=gain, op0=ALU.add, op1=ALU.mult)
                        v.scalar_tensor_tensor(out=cb[:, t], in0=scale, scalar=1.0, in1=bias, op0=ALU.add, op1=ALU.mult)
                        dve.drain()
                        v.tensor_tensor(cb[:, t], cb[:, t], shift, ALU.add)
                        v.tensor_scalar(ag[:, t, :], ln_rows(2 * (1 - n), l - 1 + n), ALPHA, None, ALU.mult)
                        v.tensor_scalar(ab[:, t, :], ln_rows(2 * (1 - n) + 1, l - 1 + n), ALPHA, None, ALU.mult)
                    else:
                        v.tensor_scalar(cs[:, t], scale, 1.0, None, ALU.add)
                        v.tensor_copy(cb[:, t], shift)
                dve.drain()

            def statistics(h):
                cols = half_cols(h)
                v.tensor_copy(mean[:, cols], pb[:, aux(), 0:HALF]).then_inc(aux_free, 1)
                dve.drain()
                v.tensor_tensor(sqt[:, h, :], mean[:, cols], mean[:, cols], ALU.mult)
                dve.drain()
                v.tensor_tensor(rstd[:, cols], pb[:, aux(), 0:HALF], sqt[:, h, :], ALU.subtract).then_inc(aux_free, 1)
                dve.drain()
                v.tensor_scalar(rstd[:, cols], rstd[:, cols], 0.0, None, ALU.max).then_inc(var_ready, 1)
                dve.wait_ge(std_ready, ST.up())
                v.reciprocal(rstd[:, cols], rstd[:, cols])
                dve.drain()

            def normalise(x, cols, sem_):
                v.tensor_tensor(x, x, mean[:, cols], ALU.subtract)
                dve.drain()
                v.tensor_tensor(x, x, rstd[:, cols], ALU.mult).then_inc(sem_, 1)

            def samples(t):
                x = xa[:, :, SEQ:TOK]
                if t:
                    v.tensor_tensor(x, x, mean[:, SEQ:TOK].unsqueeze(1).to_broadcast([P, KT, NS]), ALU.subtract)
                    dve.drain()
                    v.tensor_tensor(x, x, rstd[:, SEQ:TOK].unsqueeze(1).to_broadcast([P, KT, NS]), ALU.mult)
                    dve.drain()
                x, o = [a.rearrange("p m (b t) -> p m b t", b=DEC_B) for a in (x, hfs[:])]
                for src, coef, op in ((x, cs, ALU.mult), (o, cb, ALU.add)):
                    v.tensor_tensor(o, src, coef[:, t, :, 1:NC].unsqueeze(3).to_broadcast([P, KT, DEC_B, DEC_T]), op)
                    dve.drain()
                split(h_hi[:, :, SEQ:TOK], h_lo[:, :, SEQ:TOK], hfs[:])

            def apply(t):
                for h in range(2):
                    w = HP if h else HALF
                    cols = slice(h * HALF, h * HALF + w)
                    if t:
                        statistics(h)
                    if h:
                        samples(t)
                    if t:
                        normalise(xa[:, 0, cols], cols, n_ready)
                    for m in range(KT):
                        if t and h == 0 and m in LATE:
                            add_product(t - 1, LATE[m], 1, True)
                        if t and m + 1 < KT:
                            normalise(xa[:, m + 1, cols], cols, n_ready)
                        dve.wait_ge(hf_ready, HF.up())
                        v.tensor_tensor(h_lo[:, m, cols], hf[:, m % 2, 0:w], h_hi[:, m, cols].bitcast(F32),
                                        ALU.subtract).then_inc(h_ready, 1)

            HF = Tally()

            def final():
                for h in range(2):
                    statistics(h)
                    for m in range(KT):
                        if h == 0 and m in LATE:
                            add_product(2 * DEPTH - 1, LATE[m], 1, True)
                        normalise(xa[:, m, half_cols(h)], half_cols(h), n_ready)

            def clear_sums():
                v.memset(s_sum[:], 0.0)
                v.memset(s_sq[:], 0.0)
                dve.drain()

            def add_sums(y, h):
                v.tensor_tensor(s_sum[:, half_cols(h)], s_sum[:, half_cols(h)], y, ALU.add)
                dve.wait_ge(sq_ready, SQ.up())
                v.tensor_tensor(s_sq[:, half_cols(h)], s_sq[:, half_cols(h)], sqt[:, h, :], ALU.add
                                ).then_inc(q_done, 1)

            def add_product(e, m, h, last):
                gp, gs = per_row(gate, e, m)
                if h:
                    dve.drain()
                dve.wait_ge(acc_ready, G.v + 1)
                if h:
                    dve.sem_inc(split_free, 1)
                ps = pb[:, G.n % BANKS, 0:HALF]
                w = HP if h else HALF
                y = one(xa, m, slice(h * HALF, h * HALF + w))
                if h:
                    v.tensor_tensor(bt(smt[:]), bt(ps[:, HP:HALF]), gs, ALU.mult)
                last_ = v.scalar_tensor_tensor(out=y, in0=ps[:, 0:w], scalar=gp, in1=y, op0=ALU.mult, op1=ALU.add)
                if h:
                    dve.drain()
                    ys = one(xa, m, slice(SEQ, TOK))
                    last_ = v.tensor_tensor(ys, ys, smt[:], ALU.add)
                last_.then_inc(acc_free, 1)
                if last:
                    dve.drain()
                    add_sums(one(xa, m, half_cols(h)), h)
                G.up()

            def down(e):
                dve.wait_ge(xa_ready, 16 * (e + 1))
                with rolled(dve, 2, (G, 8)) as i:
                    for m in range(4):
                        for h in range(2):
                            add_product(e, i * 4 + m, h, False)

            def down_norm(e):
                dve.wait_ge(xa_ready, 16 * (e + 1))
                clear_sums()
                for m in range(4):
                    for h in range(2):
                        add_product(e, m, h, True)
                for m in range(4, KT):
                    add_product(e, m, 0, True)
                add_product(e, 4, 1, True)

            def gated(m, h, q):
                dve.wait_ge(acc_ready, G.v + 2)
                if h:
                    dve.sem_inc(split_free, 2)
                dve.wait_ge(sg_ready, SG.up())
                v.tensor_tensor(pr[:, q, :], pb[:, (G.n + 1) % BANKS, 0:HALF], sg[:, q, :], ALU.mult
                                ).then_inc(acc_free, 2)
                dve.drain()
                split(one(a_hi, m, half_cols(h)), one(a_lo, m, half_cols(h)), pr[:, q, :]).then_inc(a_ready, 1)
                G.up(2)

            def gate_up(count, fresh):
                if fresh:
                    for h in range(2):
                        for m in range(2):
                            gated(m, h, m)
                with rolled(dve, count // 2 - fresh, (G, 8), (SG, 4)) as i:
                    for m in range(2):
                        for h in range(2):
                            gated(i * 2 + (m + 2 * fresh), h, h)

            def gmlp(l):
                j = l // 3
                v.memset(wss_raw[:], 0.0).then_inc(ws_zero, 1)
                with rolled(dve, 2, (G, 20), (VV, 20)) as i:
                    for gg in range(4):
                        for tt in range(TT):
                            dve.wait_ge(v_ready, VV.up())
                            if tt == TT - 1:
                                dve.sem_inc(split_free, 2)
                            v.bn_stats(one(bst[:, tt], i * 4 + gg),
                                       v_sb[:, tt, bass.ds(i * 1024 + gg * 256, 256)]).then_inc(acc_free, 1)
                            G.up()
                dve.drain()
                for tt in range(TT):
                    v.bn_aggr(bag[:, tt, :], bst[:, tt].rearrange("p g s -> p (g s)"))
                dve.drain().then_inc(var_ready, 1)
                dve.wait_ge(ws_in, 160 * (j + 1))
                v.tensor_tensor(ws_raw[:], ws_raw[:], tril[:].unsqueeze(1).to_broadcast([P, GROUPS, P]), ALU.mult)
                v.tensor_tensor(wss_raw[:, :, NS:], wss_raw[:, :, NS:],
                                tril[0:NS, 0:NS].unsqueeze(1).to_broadcast([NS, GROUPS, NS]), ALU.mult)
                dve.drain().then_inc(ws_ready, 1)
                dve.wait_ge(std_ready, ST.up())
                v.reciprocal(vrs[:], vrs[:])
                dve.drain()
                for q in range(2):
                    v.tensor_copy(wsT[:, 4 * q:4 * q + 4, :].rearrange("p g t -> p (g t)"), pb[:, aux(), :]
                                  ).then_inc(aux_free, 1)
                v.tensor_copy(wssT[:].rearrange("p g t -> p (g t)"), pb[:, aux(), :]).then_inc(aux_free, 1)
                for ph in range(2):
                    with rolled(dve, 2, (G, 8), (X, 8), (SG, 8), (GB[0], 48), (GB[1], 48), (VO, 16)) as i:
                        for gg in range(2):
                            g = i * 2 + (4 * ph + gg)
                            dve.wait_ge(gb_full[gg], GB[gg].up(48))
                            dve.wait_ge(vo_done[gg], VO.v + 16)
                            for tt in range(TT):
                                v.tensor_scalar(vn[:, gg, tt, :], v_sb[:, tt, bass.ds(g * 256, 256)],
                                                bag[:, tt, 0:1], vrs[:, tt:tt + 1], ALU.subtract, ALU.mult)
                            for n, op in enumerate((ALU.mult, ALU.add)):
                                dve.drain()
                                last_ = v.tensor_tensor(vn[:, gg], vn[:, gg],
                                                        gbt[:, gg, n, :].unsqueeze(1).to_broadcast([P, TT, 256]), op)
                            last_.then_inc(vn_ready, 1)
                            for mt in range(2):
                                m = i * 4 + (2 * gg + mt)
                                bp, bs_ = aux(), aux()
                                dve.wait_ge(aux_ready, X.v)
                                pp = pb[:, bp, :].rearrange("p (c t) -> p c t", c=4)
                                v.tensor_tensor(pp, pp, bsb[:, gg, :].unsqueeze(1).to_broadcast([P, 4, P]), ALU.add)
                                ps = bt(pb[:, bs_, 0:NS])
                                v.tensor_tensor(ps, ps, bsb[:, gg, 0:DEC_T].unsqueeze(1)
                                                .to_broadcast([P, DEC_B, DEC_T]), ALU.add)
                                dve.drain()
                                for h in range(2):
                                    dve.wait_ge(sg_ready, SG.up())
                                    if h:
                                        dve.sem_inc(split_free, 1)
                                    if h == 0:
                                        v.tensor_tensor(u_sb[:, 0:HALF], u_sb[:, 0:HALF], pb[:, bp, 0:HALF], ALU.mult)
                                    else:
                                        v.tensor_tensor(u_sb[:, HALF:SEQ], u_sb[:, HALF:SEQ], pb[:, bp, HALF:SEQ],
                                                        ALU.mult).then_inc(aux_free, 1)
                                        v.tensor_tensor(u_sb[:, SEQ:], u_sb[:, SEQ:], pb[:, bs_, 0:NS], ALU.mult
                                                        ).then_inc(aux_free, 1)
                                    dve.drain().then_inc(acc_free, 1)
                                    split(one(a_hi, m, half_cols(h)), one(a_lo, m, half_cols(h)), u_sb[:, half_cols(h)]
                                          ).then_inc(a_ready, 1)
                                    G.up()
                            if gg:
                                VO.up(16)
                    if ph:
                        for n in range(2):
                            dve.wait_ge(vo_done[n], VO.v + 16)
                    (down_norm if ph else down)(2 * l)

            VV, VO = Tally(), Tally()

            def conv(l):
                v.memset(full[:, :, 0:CTX], 0.0)
                v.tensor_copy(wdT[:].rearrange("p k w -> p (k w)"), pb[:, aux(), 0:KT * CW]).then_inc(aux_free, 1)
                for m in range(KT):
                    v.tensor_copy(stT[:, m, :], pb[:, aux(), 0:DEC_B * CTX]).then_inc(aux_free, 1)
                dve.drain().then_inc(wd_ready, 1)
                clear_sums()
                with rolled(dve, 4, (G, 8), (X, 4), (SG, 4), (SQ, 4)) as i:
                    for mm_ in range(2):
                        m = i * 2 + mm_
                        fs = full_s(full[:, mm_, :])
                        v.tensor_copy(fs[:, :, 0:CTX], one(stT, m).rearrange("p (b r) -> p b r", b=DEC_B))
                        b1 = one1(par, m, C_PW1)
                        for h in range(2):
                            dve.wait_ge(acc_ready, G.v + 2)
                            if h:
                                dve.sem_inc(split_free, 2)
                            dve.wait_ge(sg_ready, SG.up())
                            ps = pb[:, G.n % BANKS, 0:HALF]
                            w = HALF if h == 0 else HP
                            if h:
                                v.scalar_tensor_tensor(out=snew[:, mm_, :], in0=ps[:, HP:HALF], scalar=b1,
                                                       in1=sg[:, 1, HP:HALF], op0=ALU.add, op1=ALU.mult)
                            v.scalar_tensor_tensor(out=full[:, mm_, CTX + h * HALF:CTX + h * HALF + w],
                                                   in0=ps[:, 0:w], scalar=b1, in1=sg[:, h, 0:w],
                                                   op0=ALU.add, op1=ALU.mult).then_inc(acc_free, 2)
                            G.up(2)
                        dve.drain()
                        v.tensor_copy(fs[:, :, CTX:], bt(snew[:, mm_, :]))
                        dve.drain().then_inc(full_ready, 1)
                        yp, ys = one(yc, m, slice(0, SEQ)), bt(one(yc, m, slice(SEQ, TOK)))
                        bd = one1(par, m, C_DW)
                        win = fs[:, :, 0:DEC_T]
                        win = bass.AP(tensor=win.tensor, offset=win.offset, ap=[*win.ap, [1, CW]])
                        v.tensor_tensor(prod[:], win, one(wdT, m).unsqueeze(1).unsqueeze(1)
                                        .to_broadcast([P, DEC_B, DEC_T, CW]), ALU.mult)
                        v.tensor_scalar(yp, full[:, mm_, PE_TAPS:PE_TAPS + SEQ],
                                        one(wdT, m, slice(PE_TAPS, PE_TAPS + 1)), bd, ALU.mult, ALU.add)
                        dve.drain()
                        v.reduce_sum(ys, prod[:], AX.X)
                        for k in range(PE_TAPS + 1, CW):
                            v.scalar_tensor_tensor(out=yp, in0=full[:, mm_, k:k + SEQ],
                                                   scalar=one(wdT, m, slice(k, k + 1)), in1=yp,
                                                   op0=ALU.mult, op1=ALU.add)
                            dve.drain()
                        v.tensor_tensor(yp, yp, pb[:, aux(), :], ALU.add).then_inc(aux_free, 1)
                        v.tensor_scalar(ys, ys, bd, None, ALU.add)
                        dve.drain().then_inc(yc_ready, 1)
                        b = aux()
                        for dst, n, c0 in ((st_p, CTX, 0), (st_s, NS, P)):
                            last_ = v.tensor_copy(dst[:, bass.ds(m * P, P)], pb[0:n, b, c0:c0 + P])
                        last_.then_inc(aux_free, 1)
                    for mm_ in range(2):
                        for h in range(2):
                            add_sums(one(yc, i * 2 + mm_, half_cols(h)), h)
                        dve.drain()
                dve.drain().then_inc(st_ready, 1)
                dve.wait_ge(xa_ready, 16 * (2 * l + 1))
                v.tensor_tensor(gbw[:], gate[:, 2 * l], par[:, C_PW2:C_PW2 + KT].unsqueeze(2)
                                .to_broadcast([P, KT, NC]), ALU.mult)
                dve.drain()
                for m in range(KT):
                    v.tensor_scalar(xa[:, m, 0:SEQ], xa[:, m, 0:SEQ], gbw[:, m, 0:1], None, ALU.add)
                    v.tensor_tensor(bt(xa[:, m, SEQ:]), bt(xa[:, m, SEQ:]),
                                    gbw[:, m, 1:NC].unsqueeze(2).to_broadcast([P, DEC_B, DEC_T]), ALU.add)
                for h in range(2):
                    statistics(h)
                    cols = half_cols(h)
                    normalise(yc[:, 0, cols], cols, yc_ready)
                    for m in range(KT):
                        if m + 1 < KT:
                            normalise(yc[:, m + 1, cols], cols, yc_ready)
                        dve.wait_ge(hf_ready, HF.up())
                        v.tensor_tensor(a_lo[:, m, cols], hf[:, m % 2, :], a_hi[:, m, cols].bitcast(F32), ALU.subtract
                                        ).then_inc(a_ready, 1)
                down_norm(2 * l)

            def mla(l):
                half = ROPE // 2
                for c0, n in DCH:
                    for tt in range(TT):
                        dve.wait_ge(acc_ready, G.v + 1)
                        if tt == TT - 1:
                            dve.sem_inc(split_free, 2)
                        v.tensor_copy(dtok[:, tt, c0:c0 + n], pb[:, G.n % BANKS, 0:n]).then_inc(acc_free, 1)
                        G.up()
                dve.drain().then_inc(d_ready, 1)
                for q in range(4):
                    v.tensor_copy(ukT[:, 2 * q:2 * q + 2, :].rearrange("p h c -> p (h c)"), pb[:, aux(), :]
                                  ).then_inc(aux_free, 1)
                dve.wait_ge(mla_in, 64)
                dve.wait_ge(ssq_ready, 1)
                v.reciprocal(ssq[:], ssq[:])
                dve.drain()
                for tt in range(TT):
                    v.scalar_tensor_tensor(out=dtok[:, tt, 0:QR], in0=dtok[:, tt, 0:QR], scalar=ssq[:, tt, 0:1],
                                           in1=gqk[:, 0:QR], op0=ALU.mult, op1=ALU.mult)
                    v.scalar_tensor_tensor(out=ckv[:, tt, :], in0=dtok[:, tt, QR:QR + KVR], scalar=ssq[:, tt, 1:2],
                                           in1=gqk[:, QR:], op0=ALU.mult, op1=ALU.mult)
                cos, sin = rtab[:, :, 0:half], rtab[:, :, half:]
                x1, x2 = dtok[:, :, QR + KVR:QR + KVR + half], dtok[:, :, QR + KVR + half:]
                ra, rb = [rt[:, n, 0:TT * half].rearrange("p (t r) -> p t r", t=TT) for n in range(2)]
                v.tensor_tensor(ra, x1, cos, ALU.mult)
                v.tensor_tensor(rb, x2, sin, ALU.mult)
                dve.drain()
                v.tensor_tensor(kr2[:, :, 0, 0:half], ra, rb, ALU.subtract)
                dve.drain()
                v.tensor_tensor(ra, x2, cos, ALU.mult)
                v.tensor_tensor(rb, x1, sin, ALU.mult)
                dve.drain()
                v.tensor_tensor(kr2[:, :, 0, half:], ra, rb, ALU.add)
                dve.drain()
                v.tensor_copy(kr2[:, :, 1, :], kr2[:, :, 0, :])
                dve.drain().then_inc(kv_ready, 1)
                for k in range(6):
                    for n, (cols, src) in enumerate(((slice(0, SEQ), slice(0, SEQ)), (slice(SEQ, TOK), slice(NS, P)))):
                        ps = pb[:, aux(), src]
                        if k < 3:
                            split(ql_hi[:, k, cols], ql_lo[:, k, cols], ps).then_inc(aux_free, 1)
                        else:
                            v.tensor_copy(ckvT[:, k - 3, cols] if k < 5 else krT[:, cols], ps).then_inc(aux_free, 1)
                dve.drain().then_inc(lat_ready, 1)
                for c in range(2):
                    for tt in range(TT):
                        dve.wait_ge(acc_ready, G.v + 1)
                        if tt == TT - 1:
                            dve.sem_inc(split_free, 1)
                        v.tensor_copy(qrt[:, tt, c * 256:(c + 1) * 256], pb[:, G.n % BANKS, 0:256]
                                      ).then_inc(acc_free, 1)
                        G.up()

                def rotate(tt):
                    q4 = qrt[:, tt, :].rearrange("p (h r) -> p h r", h=HEADS)
                    x1, x2 = q4[:, :, 0:half], q4[:, :, half:]
                    ra, rb = [rt[:, n, :].rearrange("p (h r) -> p h r", h=HEADS) for n in range(2)]
                    cos, sin = [rtab[:, tt, n * half:(n + 1) * half].unsqueeze(1).to_broadcast([P, HEADS, half])
                                for n in range(2)]
                    dve.drain()
                    v.tensor_tensor(ra, x1, cos, ALU.mult)
                    v.tensor_tensor(rb, x2, sin, ALU.mult)
                    dve.drain()
                    v.tensor_tensor(ra, ra, rb, ALU.subtract)
                    v.tensor_tensor(x2, x2, cos, ALU.mult)
                    dve.drain()
                    v.tensor_tensor(rb, x1, sin, ALU.mult)
                    dve.drain()
                    v.tensor_tensor(x2, x2, rb, ALU.add)
                    v.tensor_copy(x1, ra)

                def evac_q(h, hf_):
                    dve.wait_ge(acc_ready, G.v + 1)
                    if hf_:
                        dve.sem_inc(split_free, 1)
                    v.tensor_copy(qn[:, h % 2, half_cols(hf_)], pb[:, G.n % BANKS, 0:HALF]).then_inc(acc_free, 1)
                    G.up()

                def evac_absorbed(h):
                    for c in range(2):
                        for hf_ in range(2):
                            dve.wait_ge(acc_ready, G.v + 1)
                            ps = pb[:, G.n % BANKS, 0:HALF]
                            w = HP if hf_ else HALF
                            if hf_:
                                v.tensor_copy(qas[:, c, :, h, :], bt(ps[:, HP:]))
                            v.tensor_copy(qaT[:, c, h, hf_ * HALF:hf_ * HALF + w], ps[:, 0:w]).then_inc(acc_free, 1)
                            G.up()

                for h in range(HEADS):
                    for hf_ in range(2):
                        evac_q(h, hf_)
                    if h:
                        evac_absorbed(h - 1)
                    if h < TT:
                        rotate(h)
                    elif h == TT:
                        dve.drain().then_inc(qr_ready, 1)
                evac_absorbed(HEADS - 1)
                for q in range(4):
                    v.tensor_copy(qrT[:, q, 0:SEQ], pb[:, aux(), :]).then_inc(aux_free, 1)
                    v.tensor_copy(qrT[:, q, SEQ:], pb[:, aux(), NS:P]).then_inc(aux_free, 1)
                for q in range(2):
                    ps = pb[0:ROPE, aux(), :].rearrange("p (h t) -> p h t", h=4)
                    for i in range(4):
                        last_ = v.tensor_copy(qrs[:, :, 4 * q + i, :], bt(ps[:, i, NS:]))
                    last_.then_inc(aux_free, 1)
                dve.wait_ge(mask_in, 32)
                NA = 4 * HEADS

                def maxima(n):
                    qb = n // HEADS
                    dve.wait_ge(sc_ready, n + 1)
                    ps = pb[:, 4 + n % 2, :]
                    diag = ps[:, qb * P:(qb + 1) * P]
                    v.tensor_tensor(diag, diag, cmask[:], ALU.add)
                    dve.drain()
                    v.reduce_max(att[:, n % 2, 3:4], ps[:, 0:(qb + 1) * P], AX.X)
                    dve.drain()
                    v.tensor_scalar(att[:, n % 2, 0:1], att[:, n % 2, 3:4], -SCALE, None, ALU.mult
                                    ).then_inc(nm_ready, 1)

                def scale_rows(n):
                    N = (n // HEADS + 1) * P
                    dve.wait_ge(sc_free, n + 1)
                    v.reciprocal(att[:, n % 2, 2:3], att[:, n % 2, 1:2])
                    dve.drain()
                    v.tensor_scalar(pexp[:, n % 2, 0:N], pexp[:, n % 2, 0:N], att[:, n % 2, 2:3], None, ALU.mult
                                    ).then_inc(p_ready, 1)

                def evac_context(n):
                    qb, h = divmod(n, HEADS)
                    dve.wait_ge(acc_ready, G.v + 1)
                    v.tensor_copy(qaT[:, :, h, qb * P:(qb + 1) * P],
                                  pb[:, G.n % BANKS, 0:2 * P].rearrange("p (c q) -> p c q", c=2)).then_inc(acc_free, 1)
                    G.up()

                maxima(0)
                for n in range(NA):
                    if n + 1 < NA:
                        maxima(n + 1)
                    scale_rows(n)
                    if n:
                        evac_context(n - 1)
                evac_context(NA - 1)
                def evac_pages():
                    for dst in [pgT[:, c, q * 512:(q + 1) * 512] for c in range(2) for q in range(2)] + [
                            pgrT[:, q * 512:(q + 1) * 512] for q in range(2)]:
                        dve.wait_ge(acc_ready, G.v + 1)
                        v.tensor_copy(dst, pb[0:dst.shape[0], G.n % BANKS, :]).then_inc(acc_free, 1)
                        G.up()

                def evac_sample_context(b):
                    bk = aux()
                    for c in range(2):
                        last_ = v.tensor_copy(qaT[:, c, :, SEQ + DEC_T * b:SEQ + DEC_T * (b + 1)],
                                              pb[:, bk, c * R:(c + 1) * R].rearrange("p (h t) -> p h t", h=HEADS))
                    last_.then_inc(aux_free, 1)

                evac_pages()
                for b in range(DEC_B):
                    banks = [aux() for _ in range(3)]
                    assert banks == [SAMPLE_BANK(b, q) for q in range(3)]
                    m_ = pb[0:R, banks[2], 0:P]
                    v.tensor_tensor(m_, m_, smask[:, b, :], ALU.add)
                    dve.drain()
                    for q in range(3):
                        v.reduce_max(satt[:, 5 + q:6 + q], pb[0:R, banks[q], 0:512 if q < 2 else P], AX.X)
                    dve.drain()
                    v.reduce_max(satt[:, 4:5], satt[:, 5:8], AX.X)
                    dve.drain()
                    v.tensor_scalar(satt[:, 0:1], satt[:, 4:5], -SCALE, None, ALU.mult).then_inc(nm_ready, 1)
                    if b + 1 < DEC_B:
                        evac_pages()
                    dve.wait_ge(se_ready, b + 1)
                    v.reduce_sum(satt[:, 4:5], satt[:, 1:4], AX.X)
                    dve.drain()
                    v.reciprocal(satt[:, 4:5], satt[:, 4:5])
                    dve.drain()
                    v.tensor_scalar(sp_[:], sp_[:], satt[:, 4:5], None, ALU.mult).then_inc(aux_free, 3)
                    if b:
                        evac_sample_context(b - 1)
                    v.tensor_copy(spT[:, 0:8, :].rearrange("p g r -> p (g r)"), pb[:, aux(), :]).then_inc(aux_free, 1)
                    v.tensor_copy(spT[:, 8, :], pb[:, aux(), 0:R]).then_inc(aux_free, 1)
                    v.tensor_copy(scx[:], pb[0:R, aux(), 0:KVR]).then_inc(aux_free, 1)
                    dve.drain().then_inc(pg_used, 1)
                evac_sample_context(DEC_B - 1)
                for h in range(HEADS):
                    for hf_ in range(2):
                        dve.wait_ge(acc_ready, G.v + 1)
                        split(a_hi[:, h, half_cols(hf_)], a_lo[:, h, half_cols(hf_)], pb[:, G.n % BANKS, 0:HALF]
                              ).then_inc(acc_free, 1)
                        dve.drain().then_inc(a_ready, 1)
                        G.up()
                dve.wait_ge(kv_out, 64)
                down_norm(2 * l)

            modulation(0)
            dve.drain().then_inc(coef_ready, 1)
            dve.drain().then_inc(n_ready, 16)
            apply(0)
            for l in range(1, DEPTH):
                modulation(l)
            v.tensor_copy(ag[:, 2 * DEPTH, :], ln_rows(2, DEPTH - 1))
            v.tensor_copy(ab[:, 2 * DEPTH, :], ln_rows(3, DEPTH - 1))
            dve.drain()
            for l in range(DEPTH):
                (gmlp, conv, mla)[l % 3](l)
                apply(2 * l + 1)
                for n, (first, count) in enumerate(GU):
                    gate_up(count, n == 0)
                    (down_norm if n == 2 else down)(2 * l + 1)
                if l < DEPTH - 1:
                    apply(2 * l + 2)
                else:
                    final()
            for tt in range(TT):
                n = P if tt < 4 else NS
                if tt >= 2:
                    dve.wait_ge(y_out[tt % 2], 16 * (tt // 2))
                for q in range(2):
                    v.tensor_copy(yo[0:n, tt % 2, q * 512:(q + 1) * 512], pb[0:n, aux(), :]).then_inc(aux_free, 1)
                dve.drain().then_inc(yo_ready, 1)


INS = ["x_prompt", "x_sample", "cache_ckv", "cache_krope", "state_conv", "page_table", "c_prompt", "c_sample",
       "ada_w", "ada_b", "ln_mix_g", "ln_mix_b", "ln_ffn_g", "ln_ffn_b", "ffn_w_gate", "ffn_w_up", "ffn_w_down",
       "gmlp_w_in", "gmlp_ln_g", "gmlp_ln_b", "gmlp_w_s", "gmlp_b_s", "gmlp_w_out",
       "conv_w_pw1", "conv_b_pw1", "conv_w_dw", "conv_b_dw", "conv_ln_g", "conv_ln_b", "conv_w_pw2", "conv_b_pw2",
       "mla_w_down", "mla_g_q", "mla_g_kv", "mla_w_uq", "mla_w_uk", "mla_w_uv", "mla_w_o"]
OUTS_ = {
    "y_prompt": (1, SEQ, D), "y_sample": (DEC_B, DEC_T, D),
    "new_ckv_prompt": (1, 1, SEQ, KVR), "new_krope_prompt": (1, 1, SEQ, ROPE),
    "new_ckv_sample": (1, DEC_B, DEC_T, KVR), "new_krope_sample": (1, DEC_B, DEC_T, ROPE),
    "new_conv_prompt": (1, 1, CTX, D), "new_conv_sample": (1, DEC_B, CTX, D),
    "new_gmlp_v_sample": (2, DEC_B, DEC_T, GDIM),
}


def constants():
    f = np.float32
    q, k = np.arange(P)[:, None], np.arange(P)[None, :]
    causal = np.where(k <= q, 0.0, NEG).astype(f)
    row = np.arange(HEADS * DEC_T) % DEC_T
    col = np.arange(P) - NS
    smask = np.full((HEADS * DEC_T, DEC_B, P), NEG, f)
    for b in range(DEC_B):
        ok = (col[None, :] >= 0) & (col[None, :] // DEC_T == b) & (col[None, :] % DEC_T <= row[:, None])
        smask[:, b][ok] = 0.0
    pos = np.zeros((P, TT), f)
    for t in range(TT - 1):
        pos[:, t] = t * P + np.arange(P)
    pos[:, TT - 1] = np.where(col >= 0, PAST + col % DEC_T, SEQ + col)
    half = ROPE // 2
    inv = (f(10000.0) ** (-np.arange(half, dtype=f) / f(half))).astype(f)
    ang = (pos[:, :, None] * inv).astype(f).astype(np.float64)
    rope = np.concatenate([np.cos(ang), np.sin(ang)], -1).astype(f)
    return {"c_ident": np.eye(P, dtype=f), "c_tril": (k <= q).astype(f), "c_causal": causal,
            "c_smask": smask, "c_rope": rope}


def kernel(**inputs):
    import concourse.bacc as bacc
    from concourse.bass_utils import run_bass_kernel_spmd

    nc = bacc.Bacc("TRN2", target_bir_lowering=False, num_devices=1)
    arrays = {n: np.ascontiguousarray(inputs[n]) for n in INS} | constants()
    feeds, A, O = {}, {}, {}
    for name, a in arrays.items():
        feeds["in_" + name] = a
        A[name] = nc.dram_tensor("in_" + name, a.shape, mybir.dt.from_np(a.dtype), kind="ExternalInput").ap()
    for name, shape in OUTS_.items():
        O[name] = nc.dram_tensor("out_" + name, shape, F32, kind="ExternalOutput").ap()
    trunk(nc, A, O)
    r = run_bass_kernel_spmd(nc, [feeds], core_ids=[0])
    return tuple(r.results[0]["out_" + name] for name in OUTS_)
```
